# Optimizing a Trainium2 kernel written in Bass

```python
import jax, jax.numpy as jnp
from jax import lax
import numpy as np

D_MODEL = 2048
BATCH = 1
SEQ = 256
DEPTH = 2

CHUNK = 64
N_MIXERS = 2
N_LAYERS_A = (DEPTH + 1) // 2
N_LAYERS_B = DEPTH // 2
FOX_HEADS = 16
FOX_HEAD_DIM = D_MODEL // FOX_HEADS
FOX_QKV = FOX_HEADS * FOX_HEAD_DIM
FOX_IN = 3 * FOX_QKV + FOX_HEADS
FOX_Q_BLOCK = 128
FOX_FORGET_BIAS = 3.0
SWA_Q_HEADS = 32
SWA_KV_HEADS = 4
SWA_HEAD_DIM = D_MODEL // SWA_Q_HEADS
SWA_Q = SWA_Q_HEADS * SWA_HEAD_DIM
SWA_KV = SWA_KV_HEADS * SWA_HEAD_DIM
SWA_IN = SWA_Q + 2 * SWA_KV
SWA_WINDOW = 128
SWA_WIN_CHUNKS = SWA_WINDOW // CHUNK
ROPE_THETA = 10000.0
D_FF = 11 * D_MODEL // 4
CONV_WIDTH = 3
EPS = 1e-6

kernel_name = "fox_swa_sink_convglu_hybrid"

def rms_norm(x, g):
    xf = x.astype(jnp.float32)
    y = xf * lax.rsqrt(jnp.mean(xf * xf, axis=-1, keepdims=True) + EPS)
    return (y * g.astype(jnp.float32)).astype(x.dtype)

def rope(x, pos):
    d = x.shape[-1]
    half = d // 2
    inv_freq = ROPE_THETA ** (-jnp.arange(half, dtype=jnp.float32) / half)
    ang = pos.astype(jnp.float32)[:, None] * inv_freq[None, :]
    cos = jnp.cos(ang)[:, None, :]
    sin = jnp.sin(ang)[:, None, :]
    xf = x.astype(jnp.float32)
    x1, x2 = xf[..., :half], xf[..., half:]
    return jnp.concatenate([x1 * cos - x2 * sin, x2 * cos + x1 * sin], axis=-1).astype(x.dtype)

def forgetting_attention(q, k, v, log_f):
    b, s, h, d = q.shape
    nqb = s // FOX_Q_BLOCK
    scale = d ** -0.5
    c = jnp.cumsum(log_f, axis=1)
    c_k = c.transpose(0, 2, 1)[:, :, None, :]
    k_pos = jnp.arange(s)
    q_blocks = q.reshape(b, nqb, FOX_Q_BLOCK, h, d).transpose(1, 0, 2, 3, 4)
    c_blocks = c.reshape(b, nqb, FOX_Q_BLOCK, h).transpose(1, 0, 3, 2)
    q_pos = k_pos.reshape(nqb, FOX_Q_BLOCK)

    def one_block(args):
        qi, ci, pi = args
        logits = jnp.einsum('bqhd,bkhd->bhqk', qi, k).astype(jnp.float32) * scale
        logits = logits + (ci[..., None] - c_k)
        causal = pi[:, None] >= k_pos[None, :]
        logits = jnp.where(causal, logits, -jnp.inf)
        p = jax.nn.softmax(logits, axis=-1).astype(v.dtype)
        return jnp.einsum('bhqk,bkhd->bqhd', p, v)

    out = lax.map(one_block, (q_blocks, c_blocks, q_pos))
    return out.transpose(1, 0, 2, 3, 4).reshape(b, s, h, d)

def shift_chunks(xc, n):
    if n == 0:
        return xc
    nc = xc.shape[1]
    return jnp.pad(xc, ((0, 0), (n, 0), (0, 0), (0, 0), (0, 0)))[:, :nc]

def sliding_window_sink_attention(q, k, v, sinks):
    b, s, hq, d = q.shape
    hkv = k.shape[2]
    g = hq // hkv
    nc = s // CHUNK
    scale = d ** -0.5
    qc = q.reshape(b, nc, CHUNK, hkv, g, d)
    kc = k.reshape(b, nc, CHUNK, hkv, d)
    vc = v.reshape(b, nc, CHUNK, hkv, d)
    kw = jnp.concatenate([shift_chunks(kc, n) for n in range(SWA_WIN_CHUNKS - 1, -1, -1)], axis=2)
    vw = jnp.concatenate([shift_chunks(vc, n) for n in range(SWA_WIN_CHUNKS - 1, -1, -1)], axis=2)
    logits = jnp.einsum('bcqkgd,bcjkd->bckgqj', qc, kw).astype(jnp.float32) * scale
    lag = SWA_WIN_CHUNKS - 1 - jnp.arange(SWA_WIN_CHUNKS * CHUNK) // CHUNK
    valid = jnp.arange(nc)[:, None] >= lag[None, :]
    logits = jnp.where(valid[None, :, None, None, None, :], logits, -jnp.inf)
    sink = sinks.astype(jnp.float32).reshape(hkv, g)[None, None, :, :, None, None]
    m = jnp.maximum(jnp.max(logits, axis=-1, keepdims=True), sink)
    p = jnp.exp(logits - m)
    denom = jnp.sum(p, axis=-1, keepdims=True) + jnp.exp(sink - m)
    p = (p / denom).astype(v.dtype)
    out = jnp.einsum('bckgqj,bcjkd->bcqkgd', p, vw)
    return out.reshape(b, s, hq, d)

def fox_mixer(h, w_in, f_bias, q_g, k_g, w_out):
    b, s, _ = h.shape
    proj = h @ w_in
    q, k, v, f = jnp.split(proj, [FOX_QKV, 2 * FOX_QKV, 3 * FOX_QKV], axis=-1)
    q = rms_norm(q.reshape(b, s, FOX_HEADS, FOX_HEAD_DIM), q_g)
    k = rms_norm(k.reshape(b, s, FOX_HEADS, FOX_HEAD_DIM), k_g)
    v = v.reshape(b, s, FOX_HEADS, FOX_HEAD_DIM)
    log_f = jax.nn.log_sigmoid((f + f_bias).astype(jnp.float32))
    o = forgetting_attention(q, k, v, log_f)
    return o.reshape(b, s, FOX_QKV) @ w_out

def swa_mixer(h, w_in, q_g, k_g, sinks, w_out):
    b, s, _ = h.shape
    pos = jnp.arange(s)
    proj = h @ w_in
    q, k, v = jnp.split(proj, [SWA_Q, SWA_Q + SWA_KV], axis=-1)
    q = rope(rms_norm(q.reshape(b, s, SWA_Q_HEADS, SWA_HEAD_DIM), q_g), pos)
    k = rope(rms_norm(k.reshape(b, s, SWA_KV_HEADS, SWA_HEAD_DIM), k_g), pos)
    v = v.reshape(b, s, SWA_KV_HEADS, SWA_HEAD_DIM)
    o = sliding_window_sink_attention(q, k, v, sinks)
    return o.reshape(b, s, SWA_Q) @ w_out

def causal_depthwise_conv(x, w, bias):
    width = w.shape[0]
    s = x.shape[1]
    xp = jnp.pad(x, ((0, 0), (width - 1, 0), (0, 0)))
    y = bias
    for j in range(width):
        y = y + xp[:, j:j + s] * w[j]
    return y

def conv_glu_ffn(h, w_up, conv_w, conv_b, w_down):
    gu = h @ w_up
    gate, up = jnp.split(gu, 2, axis=-1)
    gate = causal_depthwise_conv(gate, conv_w, conv_b)
    return (jax.nn.silu(gate) * up) @ w_down

def setup_inputs(seed: int = 0) -> dict:
    key = jax.random.key(seed)
    ks = jax.random.split(key, 17)

    def normal(k, shape, scale):
        return jax.random.normal(k, shape, jnp.float32) * scale

    out_scale = (2 * DEPTH) ** -0.5
    return {
        "x": normal(ks[0], (BATCH, SEQ, D_MODEL), 1.0),
        "attn_norm": 1.0 + normal(ks[1], (DEPTH, D_MODEL), 0.1),
        "ffn_norm": 1.0 + normal(ks[2], (DEPTH, D_MODEL), 0.1),
        "fox_w_in": normal(ks[3], (N_LAYERS_A, D_MODEL, FOX_IN), D_MODEL ** -0.5),
        "fox_f_bias": FOX_FORGET_BIAS + normal(ks[4], (N_LAYERS_A, FOX_HEADS), 0.5),
        "fox_q_norm": 1.0 + normal(ks[5], (N_LAYERS_A, FOX_HEAD_DIM), 0.1),
        "fox_k_norm": 1.0 + normal(ks[6], (N_LAYERS_A, FOX_HEAD_DIM), 0.1),
        "fox_w_out": normal(ks[7], (N_LAYERS_A, FOX_QKV, D_MODEL), FOX_QKV ** -0.5 * out_scale),
        "swa_w_in": normal(ks[8], (N_LAYERS_B, D_MODEL, SWA_IN), D_MODEL ** -0.5),
        "swa_q_norm": 1.0 + normal(ks[9], (N_LAYERS_B, SWA_HEAD_DIM), 0.1),
        "swa_k_norm": 1.0 + normal(ks[10], (N_LAYERS_B, SWA_HEAD_DIM), 0.1),
        "swa_sinks": normal(ks[11], (N_LAYERS_B, SWA_Q_HEADS), 0.5),
        "swa_w_out": normal(ks[12], (N_LAYERS_B, SWA_Q, D_MODEL), SWA_Q ** -0.5 * out_scale),
        "ffn_w_up": normal(ks[13], (DEPTH, D_MODEL, 2 * D_FF), D_MODEL ** -0.5),
        "ffn_conv_w": normal(ks[14], (DEPTH, CONV_WIDTH, D_FF), CONV_WIDTH ** -0.5),
        "ffn_conv_b": normal(ks[15], (DEPTH, D_FF), 0.02),
        "ffn_w_down": normal(ks[16], (DEPTH, D_FF, D_MODEL), D_FF ** -0.5 * out_scale),
    }

def reference(x, attn_norm, ffn_norm, fox_w_in, fox_f_bias, fox_q_norm, fox_k_norm,
              fox_w_out, swa_w_in, swa_q_norm, swa_k_norm, swa_sinks, swa_w_out,
              ffn_w_up, ffn_conv_w, ffn_conv_b, ffn_w_down):
    for i in range(DEPTH):
        slot = i // N_MIXERS
        h = rms_norm(x, attn_norm[i])
        if i % N_MIXERS == 0:
            x = x + fox_mixer(h, fox_w_in[slot], fox_f_bias[slot], fox_q_norm[slot],
                              fox_k_norm[slot], fox_w_out[slot])
        else:
            x = x + swa_mixer(h, swa_w_in[slot], swa_q_norm[slot], swa_k_norm[slot],
                              swa_sinks[slot], swa_w_out[slot])
        h = rms_norm(x, ffn_norm[i])
        x = x + conv_glu_ffn(h, ffn_w_up[i], ffn_conv_w[i], ffn_conv_b[i], ffn_w_down[i])
    return x


_drawn_inputs = setup_inputs


def setup_inputs(seed=0):
    import zlib

    import numpy as np

    out = dict(_drawn_inputs(seed))
    spreads = {}
    factors = {'fox_q_norm': 3.259,
     'fox_k_norm': 3.726,
     'swa_q_norm': 7.133,
     'swa_k_norm': 7.045,
     'swa_sinks': 8.0,
     'ffn_conv_b': 6.973}
    for name, (base, spread) in spreads.items():
        noise = np.random.default_rng([zlib.crc32(name.encode()), seed]).standard_normal(out[name].shape)
        drawn = base * np.exp(spread * noise) if base else spread * noise
        out[name] = __import__('jax').numpy.asarray(drawn.astype(out[name].dtype))
    for name, factor in factors.items():
        out[name] = (out[name] * factor).astype(out[name].dtype)
    return out
```

```python
from contextlib import ExitStack

import numpy as np

import concourse.bass as bass
from concourse import mybir

F32 = mybir.dt.float32
F32R = mybir.dt.float32r
ACT = mybir.ActivationFunctionType
ALU = mybir.AluOpType
AX_X = mybir.AxisListType.X

P = 128
D = 2048
T = 256
TT = T // P
KT = D // P
FF = 11 * D // 4
FT = FF // P
LAYERS = 2
EPS = 1e-6

FOX_H, FOX_D = 16, 128
FOX_PAIRS = FOX_H // 2
SWA_H, SWA_KV, SWA_D = 32, 4, 64
SWA_GROUPS = SWA_H // 4
CHUNK = 64
NEG = -1e30

RAW = 4
UNIT = 1024
GROUP4 = 8
DOWN_UNITS = FT // 2
UP_GROUPS = FF // 512

U_F = 0
U_FOX = U_F + 2
U_FOX_OUT = U_FOX + 12 * FOX_PAIRS
U_FFN = [U_FOX_OUT + 32, 0]
U_SWA = U_FFN[0] + 2 * GROUP4 * UP_GROUPS + 4 * DOWN_UNITS
U_SWA_OUT = U_SWA + 8 + 4 * SWA_GROUPS
U_FFN[1] = U_SWA_OUT + 32
U_END = U_FFN[1] + 2 * GROUP4 * UP_GROUPS + 4 * DOWN_UNITS


def constant_table():
    i = np.arange(P)
    parts = {}
    parts["ident"] = np.eye(P)
    parts["mean_d"] = np.full((P, P), 1.0 / D)
    parts["mean_fox"] = np.full((P, P), 1.0 / FOX_D)
    parts["causal"] = np.where(i[:, None] >= i[None, :], 0.0, NEG)
    parts["mean_swa"] = (i[:, None] // SWA_D == i[None, :] // SWA_D) / SWA_D
    half = SWA_D // 2
    src = np.where(i % SWA_D < half, i + half, i - half)
    parts["swap"] = (i[:, None] == src[None, :]).astype(np.float64)
    inv = np.float32(10000.0) ** (-np.arange(half, dtype=np.float32) / np.float32(half))
    ang = np.arange(T, dtype=np.float32)[None, :] * inv.astype(np.float32)[i % half][:, None]
    parts["cos"] = np.cos(ang)
    parts["sin"] = np.sin(ang) * np.where(i % SWA_D < half, -1.0, 1.0)[:, None]
    qc = i // CHUNK
    k0 = np.arange(P) // CHUNK
    k1 = (CHUNK + np.arange(P + CHUNK)) // CHUNK
    sees = lambda q, k: np.where((k[None, :] <= q[:, None]) & (k[None, :] >= q[:, None] - 1), 0.0, NEG)
    parts["window0"] = sees(qc, k0)
    parts["window1"] = sees(qc + 2, k1)
    at, cols = {}, 0
    for name, a in parts.items():
        at[name] = (cols, cols + a.shape[1])
        cols += a.shape[1]
    return np.concatenate([a.astype(np.float32) for a in parts.values()], axis=1), at


def trunk(nc, x, attn_norm, ffn_norm, fox_w_in, fox_f_bias, fox_q_norm, fox_k_norm, fox_w_out,
          swa_w_in, swa_q_norm, swa_k_norm, swa_sinks, swa_w_out, ffn_w_up, ffn_conv_w,
          ffn_conv_b, ffn_w_down, out):
    table, col = constant_table()
    consts = nc.inline_tensor(table, name="const_table").ap()

    with ExitStack() as ctx:
        def sem(name):
            return ctx.enter_context(nc.semaphore(name))

        place = [nc.sbuf_base + (-nc.sbuf_base) % 64]

        def sb(name, shape, dt=F32, at=None):
            size = int(np.prod(shape[1:])) * 4
            size += -size % 32
            if at is None:
                at = place[0]
                place[0] += size
            assert at + size <= nc.sbuf_usable_end, (name, at + size)
            return nc.alloc_sbuf_tensor_at(name, shape, dt, offset=at)

        xT = sb("xT", [P, KT, T])
        hs = sb("hs", [P, KT, 2, T], F32R)
        raw = [sb(f"raw{s}", [P, UNIT]) for s in range(RAW)]
        whi = [sb(f"whi{s}", [P, UNIT], F32R) for s in range(RAW)]
        wlo = [sb(f"wlo{s}", [P, UNIT], F32R) for s in range(RAW)]
        ident = sb("ident", [P, P])
        mean_d = sb("mean_d", [P, P])
        gains = sb("gains", [P, 2 * LAYERS, KT])
        conv = sb("conv", [P, LAYERS, 4, FT])
        eps = sb("eps", [P, 1])
        rln = sb("rln", [P, T])
        rbc = sb("rbc", [P, T])
        hf_at = place[0]
        hf = sb("hf", [P, 4, T])
        sqt = sb("sqt", [P, 2, 2, T])
        ssacc = sb("ssacc", [P, 2, T])
        gbuf = sb("gbuf", [P, 4, T + 2])
        ybuf_at = place[0]
        ybuf = sb("ybuf", [P, 4, T])
        region = place[0]
        xin = sb("xin", [P, TT, D], at=region)
        gs = sb("gs", [P, UP_GROUPS, 4, 2, T], F32R, at=region)
        inr = [region]

        def rg(name, shape, dt=F32):
            size = int(np.prod(shape[1:])) * 4
            size += -size % 32
            inr[0] += size
            assert inr[0] <= region + FT * 2 * T * 4
            return sb(name, shape, dt, at=inr[0] - size)

        oT = rg("oT", [P, KT, 2, T], F32R)
        qs = rg("qs", [P, 2, T])
        sq = rg("sq", [P, 2, T])
        lnb = rg("lnb", [P, 2, T])
        rb = rg("rb", [P, 2, T])
        qn = rg("qn", [P, 2, 2, T])
        kn = rg("kn", [P, 2, 2, T])
        tq = rg("tq", [P, 2, T])
        t1 = rg("t1", [P, 2, T])
        t2 = rg("t2", [P, 2, T])
        kdup = rg("kdup", [P, SWA_KV, T])
        vt = rg("vt", [P, 2, TT, T])
        pr = rg("pr", [P, 4, 3, P])
        pT = rg("pT", [P, 4, 3, P])
        on = rg("on", [P, 2, TT, P])
        mean_h = rg("mean_h", [P, P])
        swap = rg("swap", [P, P])
        cos = rg("cos", [P, T])
        sin = rg("sin", [P, T])
        mask = rg("mask", [P, 320])
        mask_r = rg("mask_r", [P, 320], F32R)
        ident_r = rg("ident_r", [P, P], F32R)
        nc_k = rg("nc_k", [P, T])
        fz = rg("fz", [P, T])
        fe = rg("fe", [P, T])
        fm = rg("fm", [P, T])
        ones_t = rg("ones_t", [P, T])
        mx = rg("mx", [P, 4, 2])
        nm = rg("nm", [P, 4, 2])
        es = rg("es", [P, 4, 2])
        ls = rg("ls", [P, 4, 2])
        rl = rg("rl", [P, 4, 2])
        qg = rg("qg", [P, 1])
        kg = rg("kg", [P, 1])
        qg0 = rg("qg0", [P, 1])
        fb = rg("fb", [P, 1])
        sinks = rg("sinks", [P, SWA_H])
        small = sb("small", [FT, 4 * LAYERS, P], at=ybuf_at)
        grow = sb("grow", [KT, 2 * LAYERS, P], at=hf_at)

        ps = ctx.enter_context(nc.psum_tensor("ps", [P, 8, 512], F32))

        w_land = [sem(f"w_land{s}") for s in range(RAW)]
        x_land = [sem(f"x_land{t}") for t in range(TT)]
        c_land = sem("c_land")
        f_land = sem("f_land")
        s_land = sem("s_land")
        o_land = sem("o_land")
        hi_ready = sem("hi_ready")
        lo_ready = sem("lo_ready")
        unit_done = sem("unit_done")
        v_set = sem("v_set")
        p_tab = sem("p_tab")
        v_tab = sem("v_tab")
        p_x = sem("p_x")
        v_x = sem("v_x")
        a_sqx = sem("a_sqx")
        v_ss = sem("v_ss")
        p_ss = sem("p_ss")
        a_rln = sem("a_rln")
        a_r = sem("a_r")
        v_h = sem("v_h")
        a_hh = sem("a_hh")
        v_hl = sem("v_hl")
        v_x1 = sem("v_x1")
        a_fz = sem("a_fz")
        v_f = sem("v_f")
        a_f = sem("a_f")
        v_c = sem("v_c")
        a_cst = sem("a_cst")
        v_gain = sem("v_gain")
        a_half = sem("a_half")
        v_qs = sem("v_qs")
        a_sq = sem("a_sq")
        p_ssq = sem("p_ssq")
        a_ln = sem("a_ln")
        a_rk = sem("a_rk")
        v_qn = sem("v_qn")
        p_rot = sem("p_rot")
        v_rope = sem("v_rope")
        v_qr = sem("v_qr")
        a_kd = sem("a_kd")
        a_v = sem("a_v")
        p_s = sem("p_s")
        v_mx = sem("v_mx")
        v_nm = sem("v_nm")
        a_ex = sem("a_ex")
        v_l = sem("v_l")
        v_rl = sem("v_rl")
        p_pt = sem("p_pt")
        a_pt = sem("a_pt")
        p_pv = sem("p_pv")
        v_on = sem("v_on")
        p_ot = sem("p_ot")
        a_oh = sem("a_oh")
        v_ol = sem("v_ol")
        a_g = sem("a_g")
        v_gate = sem("v_gate")
        v_tap = sem("v_tap")
        a_silu = sem("a_silu")
        a_u = sem("a_u")
        v_up = sem("v_up")
        v_gu = sem("v_gu")
        a_gh = sem("a_gh")
        v_glo = sem("v_glo")
        p_out = sem("p_out")
        v_out = sem("v_out")

        def rows(w, k0, kk, c0, cc):
            return w[k0 * P:(k0 + kk) * P, c0:c0 + cc].rearrange("(k p) c -> p k c", p=P)

        fox_in, swa_in = fox_w_in[0], swa_w_in[0]
        fox_cols = [0, D, 2 * D]
        F0 = 3 * D + FOX_H - P

        def fox_plan():
            steps = [("unit", U_F + j, "f", 0, j) for j in range(2)] + [("f", 0)]
            for p in range(FOX_PAIRS + 1):
                a, b = 2 * (p - 1), 2 * (p - 1) + 1
                old, new = p > 0, p < FOX_PAIRS
                side = {0: [("S", a)], 1: [("S", b)], 3: [("PT", a)], 4: [("PT", b)], 6: [("PV", a)],
                        7: [("PV", b)], 8: [("OT", a)], 9: [("OT", b)]} if old else {}
                for j in range(12):
                    if new:
                        steps.append(("unit", U_FOX + 12 * p + j, "qkv"[j // 4], p, j % 4))
                    elif j in (0, 2, 4):
                        steps.append(("unit", U_FOX_OUT + j // 2, "o", 0, j // 2))
                    if new and j % 4 == 3:
                        steps.append(("evac_v", p) if j == 11 else ("evac", 2 * p + j // 4))
                    steps += side.get(j, [])
                    if new and j in (5, 9):
                        steps.append(("ssq", 2 * p + (j == 9)))
            return steps

        FOX_N = 2 * FOX_PAIRS

        def swa_plan():
            steps = [("unit", U_SWA + j, "k", 0, j) for j in range(4)] + [("evac", FOX_N)]
            steps += [("unit", U_SWA + 4, "v", 0, 0), ("unit", U_SWA + 5, "v", 0, 1), ("ssq", FOX_N)]
            steps += [("unit", U_SWA + 6, "v", 0, 2), ("rot", FOX_N), ("unit", U_SWA + 7, "v", 0, 3),
                      ("evac_v", FOX_PAIRS)]
            for i in range(SWA_GROUPS + 2):
                h2 = FOX_H + 4 * (i - 2)
                h1 = FOX_H + 4 * (i - 1)
                g1, g2 = 1 <= i <= SWA_GROUPS, i >= 2
                n1 = FOX_N + i
                side = [[], [], [], []]
                side[0] += [("S", h2 + 2), ("S", h2 + 3)] * g2 + [("ssq", n1)] * g1 + [("PT", h2), ("PT", h2 + 1)] * g2
                side[1] += [("PV", h2), ("PV", h2 + 1)] * g2 + [("rot", n1)] * g1 + [("PT", h2 + 2)] * g2
                side[2] += [("OT", h2 + 1), ("PT", h2 + 3), ("PV", h2 + 2)] * g2 + [("S", h1)] * g1
                side[3] += [("PV", h2 + 3)] * g2 + [("S", h1 + 1)] * g1 + [("OT", h2 + 3)] * g2
                for j in range(4):
                    if i < SWA_GROUPS:
                        steps.append(("unit", U_SWA + 8 + 4 * i + j, "q", i, j))
                        if j == 3:
                            steps.append(("evac", FOX_N + 1 + i))
                    elif j in (0, 2) and 2 * (i - SWA_GROUPS) + j // 2 < 3:
                        n = 2 * (i - SWA_GROUPS) + j // 2
                        steps.append(("unit", U_SWA_OUT + n, "o", 0, n))
                    steps += side[j]
            return steps

        def out_plan(base):
            return [("unit", base + n, "o", n // 4, n % 4) for n in range(3, 32)]

        def head_bank(h):
            return 4 + h % 2 if h < FOX_H else 2 + h % 4

        def proj_banks(u):
            if u < U_FOX:
                return 6
            if u < U_FOX_OUT:
                return 2 * ((u - U_FOX) // 4 % 2)
            if u < U_FFN[0]:
                return 2 * ((u - U_FOX_OUT) // 4 % 2)
            if u < U_SWA_OUT:
                return 0 if u >= U_SWA + 8 or u < U_SWA + 4 else 3
            return 2 * ((u - U_SWA_OUT) // 4 % 2)

        def norm_last(n):
            if n < FOX_N:
                return U_FOX + 12 * (n // 2) + 4 * (n % 2) + 3
            return U_SWA + 3 if n == FOX_N else U_SWA + 8 + 4 * (n - FOX_N - 1) + 3

        def norm_bank(n):
            return proj_banks(norm_last(n))

        def v_last(n):
            return U_FOX + 12 * n + 11 if n < FOX_PAIRS else U_SWA + 7

        def out_tile(h):
            if h < FOX_H:
                return h, h
            return FOX_H + (h - FOX_H) // 2, (h - FOX_H) // 2

        def on_slot(h):
            return out_tile(h)[0] % 2

        def x_pair(i, h):
            return xT[:, :, :].rearrange("p (i h k) t -> p i h k t", i=2, h=4)[:, i, h, :, :]

        X_LOAD, X_OUT0, X_DOWN0, X_OUT1, X_DOWN1 = (8 * n for n in range(5))

        block = ctx.enter_context(nc.Block())

        @block.sync
        def _(sp):
            for t in range(TT):
                sp.dma_start(xin[:, t, :], x[0, t * P:(t + 1) * P, :]).then_inc(x_land[t], 16)

            def load(u, src, slot):
                n = src.shape[1]
                if not isinstance(u, int) or u >= RAW:
                    sp.wait_ge(lo_ready, u - RAW + 1)
                sp.dma_start(raw[slot][:, :].rearrange("p (k c) -> p k c", k=n), src)\
                    .then_inc(w_land[slot], 16)

            for j in range(2):
                load(U_F + j, rows(fox_in, 8 * j, 8, F0, P), (U_F + j) % RAW)
            for p in range(FOX_PAIRS):
                for j in range(12):
                    u = U_FOX + 12 * p + j
                    load(u, rows(fox_in, 4 * (j % 4), 4, fox_cols[j // 4] + 256 * p, 256), u % RAW)
            for n in range(32):
                load(U_FOX_OUT + n, rows(fox_w_out[0], 4 * (n % 4), 4, 256 * (n // 4), 256), (U_FOX_OUT + n) % RAW)

            def ffn_loads(layer):
                base = U_FFN[layer]
                with sp.Fori(0, UP_GROUPS) as i:
                    for j in range(16):
                        w = ffn_w_up[layer].rearrange("(k p) (h g c) -> p k h g c", p=P, h=2, c=512)
                        k0 = 2 * (j % 8)
                        load(base + 16 * i + j, w[:, k0:k0 + 2, j // 8, i, :], (base + j) % RAW)
                base += 16 * UP_GROUPS
                with sp.Fori(0, 2) as i:
                    for j in range(2 * DOWN_UNITS):
                        w = ffn_w_down[layer].rearrange("(k p) (i g c) -> p k i g c", p=P, i=2, c=512)
                        k0 = 2 * (j % DOWN_UNITS)
                        load(base + 2 * DOWN_UNITS * i + j, w[:, k0:k0 + 2, i, j // DOWN_UNITS, :],
                             (base + j) % RAW)

            ffn_loads(0)
            for j in range(8):
                load(U_SWA + j, rows(swa_in, 4 * (j % 4), 4, D + 256 * (j // 4), 256), (U_SWA + j) % RAW)
            for n in range(4 * SWA_GROUPS):
                u = U_SWA + 8 + n
                load(u, rows(swa_in, 4 * (n % 4), 4, 256 * (n // 4), 256), u % RAW)
            for n in range(32):
                load(U_SWA_OUT + n, rows(swa_w_out[0], 4 * (n % 4), 4, 256 * (n // 4), 256), (U_SWA_OUT + n) % RAW)
            ffn_loads(1)
            for n in range(8):
                sp.wait_ge(v_out, n + 1)
                q, t = n // 2, n % 2
                sp.dma_start(out[0, t * P:(t + 1) * P, 512 * q:512 * q + 512],
                             xin[:, t, 512 * q:512 * q + 512]).then_inc(o_land, 16)
            sp.wait_ge(o_land, 8 * 16)

        @block.scalar
        def _(act):
            cs = lambda name: consts[:, col[name][0]:col[name][1]]
            act.preload_act_table_set("natural_log_exp_and_others")
            act.dma_start(ident[:, :], cs("ident")).then_inc(c_land, 16)
            act.dma_start(mean_d[:, :], cs("mean_d")).then_inc(c_land, 16)
            for n, g in enumerate((attn_norm, ffn_norm)):
                act.dma_start(grow[:, 2 * n:2 * n + 2, :], g.rearrange("l (k p) -> k l p", p=P)).then_inc(c_land, 16)
            for l in range(LAYERS):
                act.dma_start(small[:, 4 * l:4 * l + 3, :],
                              ffn_conv_w[l].rearrange("j (f p) -> f j p", p=P)).then_inc(c_land, 16)
                act.dma_start(small[:, 4 * l + 3, :], ffn_conv_b[l].rearrange("(f p) -> f p", p=P)).then_inc(c_land, 16)
            act.dma_start(mean_h[:, :], cs("mean_fox")).then_inc(f_land, 16)
            act.dma_start(mask[:, 0:P], cs("causal")).then_inc(f_land, 16)
            act.dma_start(qg0[:, :], fox_q_norm[0].rearrange("(p a) -> p a", a=1)).then_inc(f_land, 16)
            act.dma_start(kg[:, :], fox_k_norm[0].rearrange("(p a) -> p a", a=1)).then_inc(f_land, 16)
            act.wait_ge(v_set, 4)
            act.dma_start(fb[112:128, :], fox_f_bias[0].rearrange("(p a) -> p a", a=1)).then_inc(f_land, 16)

            def conv_hi(u, slot, skip=0):
                n = u - slot if isinstance(u, int) else None
                if isinstance(u, int):
                    act.wait_ge(w_land[slot], 16 * (u // RAW + 1))
                    if u >= RAW:
                        act.wait_ge(unit_done, u - RAW + 1)
                act.activation(whi[slot][:, :], raw[slot][:, :], ACT.Copy).then_inc(hi_ready, 1)

            def conv_hi_loop(first, step, i, j):
                u0 = first + j
                act.wait_ge(w_land[u0 % RAW], (step // RAW * 16) * i + 16 * (u0 // RAW + 1))
                act.wait_ge(unit_done, step * i + (u0 - RAW + 1))
                act.activation(whi[u0 % RAW][:, :], raw[u0 % RAW][:, :], ACT.Copy).then_inc(hi_ready, 1)

            def square_x(n, pair):
                act.wait_ge(v_x, n + 1)
                if n >= 2:
                    act.wait_ge(v_ss, n - 1)
                act.activation(sqt[:, n % 2, :, :], xT[:, 2 * pair:2 * pair + 2, :], ACT.Square).then_inc(a_sqx, 1)

            def norm(n):
                act.wait_ge(p_ss, n + 1)
                act.activation(rln[:, :], ps[:, 0, 0:T], ACT.Ln, bias=eps[:, 0:1]).then_inc(a_rln, 1)
                act.wait_ge(a_rln, n + 1)
                act.activation(rbc[:, :], rln[:, :], ACT.Exp, scale=-0.5).then_inc(a_r, 1)
                for k in range(KT):
                    act.wait_ge(v_h, KT * n + k + 1)
                    act.activation(hs[:, k, 0, :], hf[:, k % 4, :], ACT.Copy).then_inc(a_hh, 1)

            def step(s):
                kind, n = s[0], s[1]
                if kind == "unit":
                    if n + RAW < U_END:
                        conv_hi(n + RAW, (n + RAW) % RAW)
                    if s[2] == "o" and s[4] == 3:
                        square_x(X_OUT0 + s[3] if n < U_FFN[0] else X_OUT1 + s[3], s[3])
                elif kind == "f":
                    act.wait_ge(unit_done, U_FOX)
                    act.wait_ge(f_land, 5 * 16)
                    act.activation(fz[96:128, :], ps[96:128, 6, 0:T], ACT.Identity, bias=fb[96:128, 0:1]).then_inc(a_fz, 1)
                    act.wait_ge(v_f, 4)
                    act.activation(fe[96:128, :], fm[96:128, :], ACT.Exp, scale=-1.0).then_inc(a_f, 1)
                    act.wait_ge(a_f, 1)
                    act.activation(fe[96:128, :], fe[96:128, :], ACT.Ln, bias=ones_t[96:128, 0:1]).then_inc(a_f, 1)
                    act.activation(mask_r[:, 0:P], mask[:, 0:P], ACT.Copy)
                    act.activation(ident_r[:, :], ident[:, :], ACT.Copy).then_inc(a_cst, 1)
                elif kind == "evac":
                    b = norm_bank(n)
                    act.wait_ge(unit_done, norm_last(n) + 1)
                    if n > 0:
                        act.wait_ge(v_qn, n)
                    act.activation(qs[:, :, :], ps[:, b:b + 2, 0:T], ACT.Copy).then_inc(a_half, 1)
                    act.wait_ge(v_qs, n + 1)
                    act.activation(sq[:, :, :], qs[:, :, :], ACT.Square).then_inc(a_sq, 1)
                elif kind == "ssq":
                    act.wait_ge(p_ssq, n + 1)
                    act.activation(lnb[:, :, :], ps[:, 7, :].rearrange("p (f t) -> p f t", f=2), ACT.Ln,
                                   bias=eps[:, 0:1]).then_inc(a_ln, 1)
                    act.wait_ge(a_ln, n + 1)
                    act.activation(rb[:, :, :], lnb[:, :, :], ACT.Exp, scale=-0.5).then_inc(a_rk, 1)
                elif kind == "rot":
                    if n == FOX_N:
                        act.wait_ge(v_qr, 1)
                        for kv in range(SWA_KV):
                            lo = SWA_D * (kv % 2)
                            src = qn[lo:lo + SWA_D, 0, kv // 2, :]
                            act.activation(kdup[0:SWA_D, kv, :], src, ACT.Copy)
                            last = act.activation(kdup[SWA_D:P, kv, :], src, ACT.Copy)
                        last.then_inc(a_kd, 1)
                elif kind == "evac_v":
                    act.wait_ge(unit_done, v_last(n) + 1)
                    if n >= 2:
                        act.wait_ge(p_pv, 2 * (n - 1))
                    b = proj_banks(v_last(n))
                    act.activation(vt[:, n % 2, :, :], ps[:, b, :].rearrange("p (t c) -> p t c", t=TT),
                                   ACT.Copy).then_inc(a_v, 1)
                elif kind == "S":
                    act.wait_ge(v_nm, n + 1)
                    if n >= 4:
                        act.wait_ge(p_pt, n - 3)
                    r, b = n % 4, head_bank(n)
                    act.activation(pr[:, r, 0, :], ps[:, b, 0:P], ACT.Exp, bias=nm[:, r, 0:1],
                                   accum_out=ls[:, r, 0:1])
                    if n < FOX_H:
                        last = act.activation(pr[:, r, 1:3, :], ps[:, b, P:3 * P].rearrange("p (a c) -> p a c", a=2),
                                              ACT.Exp, bias=nm[:, r, 1:2], accum_out=ls[:, r, 1:2])
                    else:
                        flat = pr[:, r, :, :].rearrange("p a c -> p (a c)")
                        act.wait_ge(v_set, 6)
                        act.activation(flat[:, P + CHUNK:3 * P], ps[:, b, P:P + 192], ACT.Exp,
                                       bias=nm[:, r, 1:2], accum_out=ls[:, r, 1:2])
                        last = act.activation(es[:, r, :], nm[:, r, :], ACT.Exp, bias=sinks[:, n - FOX_H:n - FOX_H + 1])
                    last.then_inc(a_ex, 1)
                elif kind == "PT":
                    act.wait_ge(p_pt, n + 1)
                    if n >= 4:
                        act.wait_ge(p_pv, n - 3)
                    act.activation(pT[:, n % 4, :, :], ps[:, 6, 0:3 * P].rearrange("p (a c) -> p a c", a=3),
                                   ACT.Copy).then_inc(a_pt, 1)
                elif kind == "OT":
                    j, k = out_tile(n)
                    act.wait_ge(p_ot, j + 1)
                    act.activation(oT[:, k, 0, :], ps[:, head_bank(n), T:2 * T], ACT.Copy).then_inc(a_oh, 1)

            def ffn(layer):
                base, it0 = U_FFN[layer], UP_GROUPS * layer
                act.preload_act_table_set("silu_and_others")
                with act.Fori(0, UP_GROUPS) as i:
                    for j in range(16):
                        conv_hi_loop(base + RAW, 16, i, j)
                        if j == 7:
                            act.wait_ge(unit_done, 16 * i + (base + 8))
                            act.wait_ge(v_tap, 3 * i + (3 * it0 + 1))
                            act.activation(gbuf[:, :, 2:T + 2], ps[:, 0:4, 0:T], ACT.Copy).then_inc(a_g, 1)
                        if j == 9:
                            act.wait_ge(v_tap, 3 * i + (3 * it0 + 4))
                            act.activation(ybuf[:, :, :], ybuf[:, :, :], ACT.Silu).then_inc(a_silu, 1)
                        if j == 15:
                            act.wait_ge(unit_done, 16 * i + (base + 16))
                            act.wait_ge(v_glo, i + (it0 + 1))
                            act.activation(hf[:, :, :], ps[:, 4:8, 0:T], ACT.Copy).then_inc(a_u, 1)
                            act.wait_ge(v_gu, i + (it0 + 1))
                            act.activation(gs[:, i, :, 0, :], hf[:, :, :], ACT.Copy).then_inc(a_gh, 1)
                act.preload_act_table_set("natural_log_exp_and_others")
                base += 16 * UP_GROUPS
                xb = X_DOWN1 if layer else X_DOWN0
                if layer == 0:
                    with act.Fori(0, 2) as i:
                        for j in range(2 * DOWN_UNITS):
                            conv_hi_loop(base + RAW, 2 * DOWN_UNITS, i, j)
                            if j % DOWN_UNITS == DOWN_UNITS - 1:
                                for h in range(2):
                                    n = xb + 2 * (j // DOWN_UNITS) + h
                                    act.wait_ge(v_x, 4 * i + (n + 1))
                                    act.wait_ge(v_ss, 4 * i + (n - 1))
                                    act.activation(sqt[:, n % 2, :, :], x_pair(i, 2 * (j // DOWN_UNITS) + h),
                                                   ACT.Square).then_inc(a_sqx, 1)
                else:
                    for u in range(base, U_END - RAW):
                        conv_hi(u + RAW, (u + RAW) % RAW)

            for u in range(RAW):
                conv_hi(u, u)
            for n in range(8):
                square_x(X_LOAD + n, n)
            norm(0)
            for s in fox_plan() + out_plan(U_FOX_OUT):
                step(s)
            norm(1)
            ffn(0)
            act.wait_ge(unit_done, U_SWA)
            for t, name in ((mean_h[:, :], "mean_swa"), (swap[:, :], "swap"), (cos[:, :], "cos"), (sin[:, :], "sin"),
                            (mask[:, 0:P], "window0"), (mask[:, P:320], "window1")):
                act.dma_start(t, cs(name)).then_inc(s_land, 16)
            for half in range(2):
                sl = slice(SWA_D * half, SWA_D * half + SWA_D)
                act.dma_start(qg0[sl, :], swa_q_norm[0].rearrange("(p a) -> p a", a=1)).then_inc(s_land, 16)
                act.dma_start(kg[sl, :], swa_k_norm[0].rearrange("(p a) -> p a", a=1)).then_inc(s_land, 16)
            act.dma_start(sinks[:, :], swa_sinks[0].partition_broadcast(P)).then_inc(s_land, 16)
            norm(2)
            act.wait_ge(s_land, 11 * 16)
            act.activation(mask_r[:, :], mask[:, :], ACT.Copy)
            act.activation(ident_r[:, :], ident[:, :], ACT.Copy).then_inc(a_cst, 1)
            for s in swa_plan() + out_plan(U_SWA_OUT):
                step(s)
            norm(3)
            ffn(1)

        @block.vector
        def _(dve):
            tt = dve.tensor_tensor

            def conv_lo(u):
                slot = u % RAW
                dve.wait_ge(hi_ready, u + 1)
                tt(wlo[slot][:, :], raw[slot][:, :], whi[slot][:, :].bitcast(F32), ALU.subtract).then_inc(lo_ready, 1)

            def conv_lo_loop(first, step_, i, j):
                u0 = first + j
                slot = u0 % RAW
                dve.wait_ge(hi_ready, step_ * i + (u0 + 1))
                tt(wlo[slot][:, :], raw[slot][:, :], whi[slot][:, :].bitcast(F32), ALU.subtract).then_inc(lo_ready, 1)

            def add_square(n):
                dve.wait_ge(a_sqx, n + 1)
                if n % 8 == 0:
                    if n:
                        dve.wait_ge(p_ss, n // 8)
                    dve.tensor_copy(ssacc[:, :, :], sqt[:, n % 2, :, :]).then_inc(v_ss, 1)
                else:
                    dve.wait_ge(v_ss, n)
                    tt(ssacc[:, :, :], ssacc[:, :, :], sqt[:, n % 2, :, :], ALU.add).then_inc(v_ss, 1)

            def residual(n, n1, xs, b, wide):
                tt(xs, xs, ps[:, b:b + wide, 0:T], ALU.add).then_inc(v_x1, 1)
                dve.wait_ge(v_x1, n1)
                tt(xs, xs, ps[:, b:b + wide, T:2 * T], ALU.add).then_inc(v_x, wide // 2)

            def norm(n):
                dve.wait_ge(a_r, n + 1)
                g = (0, 2, 1, 3)[n]
                for k in range(KT + 2):
                    if k < KT:
                        if k >= 4:
                            dve.wait_ge(v_hl, KT * n + k - 3)
                        dve.scalar_tensor_tensor(hf[:, k % 4, :], xT[:, k, :], gains[:, g, k:k + 1], rbc[:, :],
                                                 ALU.mult, ALU.mult).then_inc(v_h, 1)
                    if k >= 2:
                        dve.wait_ge(a_hh, KT * n + k - 1)
                        dve.wait_ge(v_h, KT * n + k - 1)
                        tt(hs[:, k - 2, 1, :], hf[:, (k - 2) % 4, :], hs[:, k - 2, 0, :].bitcast(F32),
                           ALU.subtract).then_inc(v_hl, 1)

            def step(s):
                kind, n = s[0], s[1]
                if kind == "unit":
                    if n + RAW < U_END:
                        conv_lo(n + RAW)
                    if s[2] == "o" and s[4] == 3:
                        xb = X_OUT0 if n < U_FFN[0] else X_OUT1
                        g = s[3]
                        dve.wait_ge(unit_done, n + 1)
                        residual(xb + g, 1 + g + (12 if n >= U_FFN[0] else 0), xT[:, 2 * g:2 * g + 2, :], proj_banks(n), 2)
                        add_square(xb + g)
                elif kind == "f":
                    r = slice(96, 128)
                    dve.wait_ge(a_fz, 1)
                    tt(fz[r, :], fz[r, :], ps[r, 6, T:2 * T], ALU.add).then_inc(v_f, 1)
                    dve.wait_ge(v_f, 1)
                    dve.memset(fz[96:112, :], 0.0).then_inc(v_f, 1)
                    dve.wait_ge(v_f, 2)
                    dve.tensor_scalar(fm[r, :], fz[r, :], -1.0, None, ALU.mult).then_inc(v_f, 1)
                    dve.wait_ge(v_f, 3)
                    tt(fm[r, :], fm[r, :], fz[r, :], ALU.max).then_inc(v_f, 1)
                    dve.wait_ge(v_f, 4)
                    dve.tensor_scalar(fz[r, :], fz[r, :], 0.0, None, ALU.min).then_inc(v_f, 1)
                    dve.wait_ge(v_f, 5)
                    dve.wait_ge(a_f, 2)
                    tt(fz[r, :], fe[r, :], fz[r, :], ALU.subtract).then_inc(v_f, 1)
                    dve.wait_ge(v_f, 6)
                    dve.tensor_tensor_scan(nc_k[r, :], ones_t[r, :], fz[r, :], 0.0, ALU.mult, ALU.add).then_inc(v_c, 1)
                    dve.tensor_scalar(qg[:, :], qg0[:, :], FOX_D ** -0.5, None, ALU.mult).then_inc(v_gain, 1)
                elif kind == "evac":
                    b = norm_bank(n)
                    dve.wait_ge(a_half, n + 1)
                    tt(qs[:, :, :], qs[:, :, :], ps[:, b:b + 2, T:2 * T], ALU.add).then_inc(v_qs, 1)
                elif kind == "ssq":
                    dve.wait_ge(a_rk, n + 1)
                    dve.wait_ge(v_qs, n + 1)
                    dve.wait_ge(v_gain, 1 if n < FOX_N else 2)
                    if n < FOX_N:
                        pair = n // 2
                        if pair >= 2:
                            dve.wait_ge(p_s, 2 * (pair - 1))
                        dst = (kn if n % 2 else qn)[:, pair % 2, :, :]
                        g = kg if n % 2 else qg
                    else:
                        dst, g = tq[:, :, :], (kg if n == FOX_N else qg)
                        if n > FOX_N:
                            dve.wait_ge(p_rot, n - FOX_N)
                    dve.scalar_tensor_tensor(dst, qs[:, :, :], g[:, 0:1], rb[:, :, :], ALU.mult, ALU.mult).then_inc(v_qn, 1)
                elif kind == "rot":
                    m = n - FOX_N
                    dve.wait_ge(v_qn, n + 1)
                    if m:
                        dve.wait_ge(v_qr, m)
                    tt(t1[:, :, :], tq[:, :, :], cos[:, None, :].to_broadcast([P, 2, T]), ALU.mult)
                    dve.wait_ge(p_rot, m + 1)
                    tt(t2[:, :, :], ps[:, 7, :].rearrange("p (f t) -> p f t", f=2),
                       sin[:, None, :].to_broadcast([P, 2, T]), ALU.mult).then_inc(v_rope, 1)
                    dve.wait_ge(v_rope, m + 1)
                    if m == 2:
                        dve.wait_ge(a_kd, 1)
                    if m >= 3:
                        dve.wait_ge(p_s, FOX_H + 4 * (m - 2))
                    tt(qn[:, m % 2, :, :], t1[:, :, :], t2[:, :, :], ALU.add).then_inc(v_qr, 1)
                elif kind == "S":
                    r, b = n % 4, head_bank(n)
                    dve.wait_ge(p_s, n + 1)
                    dve.reduce_max(mx[:, r, 0:1], ps[:, b, 0:P], AX_X)
                    end = 3 * P if n < FOX_H else P + 192
                    dve.reduce_max(mx[:, r, 1:2], ps[:, b, P:end], AX_X).then_inc(v_mx, 1)
                    dve.wait_ge(v_mx, n + 1)
                    if n < FOX_H:
                        dve.tensor_scalar(nm[:, r, :], mx[:, r, :], -1.0, None, ALU.mult).then_inc(v_nm, 1)
                    else:
                        h = n - FOX_H
                        dve.tensor_scalar(nm[:, r, :], mx[:, r, :], sinks[:, h:h + 1], -1.0, ALU.max, ALU.mult).then_inc(v_nm, 1)
                elif kind == "PT":
                    r = n % 4
                    dve.wait_ge(a_ex, n + 1)
                    if n >= FOX_H:
                        tt(ls[:, r, :], ls[:, r, :], es[:, r, :], ALU.add).then_inc(v_l, 1)
                        dve.wait_ge(v_l, n - FOX_H + 1)
                    dve.reciprocal(rl[:, r, :], ls[:, r, :]).then_inc(v_rl, 1)
                elif kind == "PV":
                    dve.wait_ge(p_pv, n + 1)
                    dve.wait_ge(v_rl, n + 1)
                    j = out_tile(n)[0]
                    if j >= 2:
                        dve.wait_ge(p_ot, j - 1)
                    dh = FOX_D if n < FOX_H else SWA_D
                    c = 0 if n < FOX_H else SWA_D * (n % 2)
                    for t in range(TT):
                        last = dve.tensor_scalar(on[:, on_slot(n), t, c:c + dh], ps[:, head_bank(n), t * dh:(t + 1) * dh],
                                                 rl[:, n % 4, t:t + 1], None, ALU.mult)
                    last.then_inc(v_on, 1)
                elif kind == "OT":
                    j, k = out_tile(n)
                    dve.wait_ge(a_oh, j + 1)
                    tt(oT[:, k, 1, :], ps[:, head_bank(n), T:2 * T], oT[:, k, 0, :].bitcast(F32),
                       ALU.subtract).then_inc(v_ol, 1)

            def ffn(layer):
                base, it0 = U_FFN[layer], UP_GROUPS * layer
                with dve.Fori(0, UP_GROUPS) as i:
                    for j in range(16):
                        conv_lo_loop(base + RAW, 16, i, j)
                        if j == 7:
                            dve.wait_ge(a_g, i + (it0 + 1))
                            tt(gbuf[:, :, 2:T + 2], gbuf[:, :, 2:T + 2], ps[:, 0:4, T:2 * T], ALU.add).then_inc(v_gate, 1)
                            dve.wait_ge(v_gate, i + (it0 + 2))
                            taps = conv[:, layer, :, :].rearrange("p w (i f) -> p w i f", f=4)
                            for w in range(3):
                                if w:
                                    dve.wait_ge(v_tap, 3 * i + (3 * it0 + w + 1))
                                for f in range(4):
                                    c = lambda m: taps[:, m, i, f:f + 1]
                                    if w == 0:
                                        last = dve.tensor_scalar(ybuf[:, f, :], gbuf[:, f, 0:T], c(0), c(3), ALU.mult, ALU.add)
                                    else:
                                        last = dve.scalar_tensor_tensor(ybuf[:, f, :], gbuf[:, f, w:w + T], c(w),
                                                                        ybuf[:, f, :], ALU.mult, ALU.add)
                                last.then_inc(v_tap, 1)
                        if j == 15:
                            dve.wait_ge(a_u, i + (it0 + 1))
                            tt(hf[:, :, :], hf[:, :, :], ps[:, 4:8, T:2 * T], ALU.add).then_inc(v_up, 1)
                            dve.wait_ge(v_up, i + (it0 + 2))
                            dve.wait_ge(a_silu, i + (it0 + 1))
                            tt(hf[:, :, :], hf[:, :, :], ybuf[:, :, :], ALU.mult).then_inc(v_gu, 1)
                            dve.wait_ge(a_gh, i + (it0 + 1))
                            tt(gs[:, i, :, 1, :], hf[:, :, :], gs[:, i, :, 0, :].bitcast(F32), ALU.subtract).then_inc(v_glo, 1)
                base += 16 * UP_GROUPS
                xb = X_DOWN1 if layer else X_DOWN0
                x1 = 8 + 12 * layer
                if layer == 0:
                    with dve.Fori(0, 2) as i:
                        for j in range(2 * DOWN_UNITS):
                            conv_lo_loop(base + RAW, 2 * DOWN_UNITS, i, j)
                            if j % DOWN_UNITS == DOWN_UNITS - 1:
                                g = j // DOWN_UNITS
                                dve.wait_ge(unit_done, 2 * DOWN_UNITS * i + (base + j + 1))
                                xs = xT[:, :, :].rearrange("p (i g k) t -> p i g k t", i=2, g=2)[:, i, g, :, :]
                                residual(None, 2 * i + (x1 + g + 1), xs, 4 * g, 4)
                                for h in range(2):
                                    n = xb + 2 * g + h
                                    dve.wait_ge(a_sqx, 4 * i + (n + 1))
                                    dve.wait_ge(v_ss, 4 * i + n)
                                    tt(ssacc[:, :, :], ssacc[:, :, :], sqt[:, n % 2, :, :], ALU.add).then_inc(v_ss, 1)
                else:
                    for u in range(base, U_END):
                        if u + RAW < U_END:
                            conv_lo(u + RAW)
                        j = u - base
                        if j % DOWN_UNITS == DOWN_UNITS - 1:
                            g = j // DOWN_UNITS
                            dve.wait_ge(unit_done, u + 1)
                            residual(None, x1 + g + 1, xT[:, 4 * g:4 * g + 4, :], 4 * (g % 2), 4)

            for free in (v_gate, v_up, v_tap, v_glo):
                dve.sem_inc(free, 1)
            dve.memset(eps[:, :], EPS).then_inc(v_set, 1)
            dve.memset(gbuf[:, :, 0:2], 0.0).then_inc(v_set, 1)
            dve.memset(ones_t[:, :], 1.0).then_inc(v_set, 1)
            dve.memset(fb[96:128, :], 0.0).then_inc(v_set, 1)
            dve.wait_ge(v_set, 4)
            dve.wait_ge(p_tab, 1)
            dve.tensor_copy(gains[:, :, :], ps[:, 7, 0:4 * KT].rearrange("p (n k) -> p n k", k=KT)).then_inc(v_tab, 1)
            dve.tensor_copy(conv[:, :, :, :], ps[:, 6, 0:8 * FT].rearrange("p (l w f) -> p l w f", l=LAYERS, w=4)).then_inc(v_tab, 1)
            for n in range(8):
                dve.wait_ge(p_x, n + 1)
                dve.tensor_copy(xT[:, 2 * n:2 * n + 2, :],
                                ps[:, n, :].rearrange("p (k t) -> p k t", k=2)).then_inc(v_x, 1)
                add_square(X_LOAD + n)
            for u in range(RAW):
                conv_lo(u)
            dve.wait_ge(v_tab, 2)
            norm(0)
            for s in fox_plan() + out_plan(U_FOX_OUT):
                step(s)
            norm(1)
            dve.wait_ge(p_ss, 2)
            dve.memset(ssacc[:, :, :], 0.0).then_inc(v_set, 1)
            dve.wait_ge(v_set, 5)
            ffn(0)
            dve.wait_ge(unit_done, U_SWA)
            dve.memset(pr[:, :, 1, 0:CHUNK], 0.0).then_inc(v_set, 1)
            dve.wait_ge(s_land, 11 * 16)
            dve.tensor_scalar(qg[:, :], qg0[:, :], SWA_D ** -0.5, None, ALU.mult).then_inc(v_gain, 1)
            norm(2)
            for s in swa_plan() + out_plan(U_SWA_OUT):
                step(s)
            norm(3)
            ffn(1)
            for n in range(8):
                dve.wait_ge(p_out, n + 1)
                q, t = n // 2, n % 2
                dve.tensor_copy(xin[:, t, 512 * q:512 * q + 512], ps[:, n, :]).then_inc(v_out, 1)

        @block.tensor
        def _(pe):
            def mm_w(slot, kj, f, width, moving, bank, first, last):
                c = (kj * width + f) * P
                hi = lambda: pe.matmul(ps[:, bank, :], whi[slot][:, c:c + P], moving.rearrange("p h t -> p (h t)"),
                                       start=first, stop=last)
                lo = lambda: pe.matmul(ps[:, bank, 0:T], wlo[slot][:, c:c + P], moving[:, 0, :], start=False, stop=False)
                if last:
                    lo()
                    return hi()
                hi()
                return lo()

            def unit(s):
                _, u, kind, g, j = s
                pe.wait_ge(lo_ready, u + 1)
                slot, b = u % RAW, proj_banks(u)
                if j == 0:
                    free_bank(s)
                if kind == "f":
                    for kj in range(8):
                        k = 8 * j + kj
                        pe.wait_ge(v_hl, k + 1)
                        last = mm_w(slot, kj, 0, 1, hs[:, k, :, :], b, k == 0, k == KT - 1)
                elif kind == "v":
                    for kj in range(4):
                        k = 4 * j + kj
                        w0 = kj * 256
                        for t in range(TT):
                            tok = slice(t * P, (t + 1) * P)
                            o = ps[:, b, t * 256:(t + 1) * 256]
                            pe.matmul(o, hs[:, k, 1, tok], whi[slot][:, w0:w0 + 256],
                                      start=k == 0 and t == 0, stop=False)
                            pe.matmul(o, hs[:, k, 0, tok], wlo[slot][:, w0:w0 + 256], start=False, stop=False)
                            last = pe.matmul(o, hs[:, k, 0, tok], whi[slot][:, w0:w0 + 256], start=False,
                                             stop=k == KT - 1 and t == TT - 1)
                else:
                    for kj in range(4):
                        k = 4 * j + kj
                        if kind == "o" and g == 0:
                            pe.wait_ge(v_ol, (0 if u < U_FFN[0] else FOX_H) + k + 1)
                        if kind != "o" and u >= U_SWA:
                            pe.wait_ge(v_hl, 2 * KT + k + 1)
                        for f in range(2):
                            src = oT if kind == "o" else hs
                            last = mm_w(slot, kj, f, 2, src[:, k, :, :], b + f, k == 0, k == KT - 1)
                last.then_inc(unit_done, 1)

            def free_bank(s):
                _, u, kind, g, j = s
                if kind == "f":
                    pe.wait_ge(v_x, 8)
                    pe.wait_ge(v_tab, 2)
                elif kind in "qkv" and u < U_FOX_OUT:
                    n = (u - U_FOX) // 4
                    if n < 2:
                        pe.wait_ge(a_r, 1)
                    else:
                        m = n - 2
                        if m % 3 == 2:
                            pe.wait_ge(a_v, m // 3 + 1)
                        else:
                            pe.wait_ge(v_qs, 2 * (m // 3) + m % 3 + 1)
                elif kind in "qkv":
                    if u < U_SWA + 4:
                        pe.wait_ge(a_r, 3)
                    elif kind == "v":
                        pe.wait_ge(v_x, X_DOWN0 + 8)
                    else:
                        pe.wait_ge(v_qs, FOX_N + 1 + g)
                else:
                    fox = u < U_FFN[0]
                    xb = X_OUT0 if fox else X_OUT1
                    if g == 0:
                        pe.wait_ge(v_qs, FOX_N if fox else FOX_N + 1 + SWA_GROUPS)
                    elif g == 1:
                        pe.wait_ge(a_v, FOX_PAIRS)
                        pe.wait_ge(v_ol, FOX_H if fox else 2 * FOX_H)
                        pe.wait_ge(v_qs, FOX_N if fox else FOX_N + 1 + SWA_GROUPS)
                    else:
                        pe.wait_ge(v_x, xb + g - 1)

            def step(s):
                kind, n = s[0], s[1]
                if kind == "unit":
                    unit(s)
                elif kind == "ssq":
                    pe.wait_ge(a_sq, n + 1)
                    if n > FOX_N:
                        pe.wait_ge(v_rope, n - FOX_N)
                    elif n > 0:
                        pe.wait_ge(a_ln, n)
                    pe.wait_ge(f_land if n < FOX_N else s_land, (5 if n < FOX_N else 11) * 16)
                    pe.matmul(ps[:, 7, :], mean_h[:, :], sq[:, :, :].rearrange("p f t -> p (f t)"),
                              start=True, stop=True).then_inc(p_ssq, 1)
                elif kind == "rot":
                    pe.wait_ge(v_qn, n + 1)
                    pe.wait_ge(a_ln, n + 1)
                    pe.matmul(ps[:, 7, :], swap[:, :], tq[:, :, :].rearrange("p f t -> p (f t)"),
                              start=True, stop=True).then_inc(p_rot, 1)
                elif kind == "S":
                    scores(n)
                elif kind == "PT":
                    pe.wait_ge(a_ex, n + 1)
                    if n > 0:
                        pe.wait_ge(a_pt, n)
                    for a in range(3):
                        last = pe.transpose(ps[:, 6, a * P:(a + 1) * P], pr[:, n % 4, a, :], ident[:, :])
                    last.then_inc(p_pt, 1)
                elif kind == "PV":
                    fox = n < FOX_H
                    pe.wait_ge(a_pt, n + 1)
                    pe.wait_ge(a_v, n // 2 + 1 if fox else FOX_PAIRS + 1)
                    dh = FOX_D if fox else SWA_D
                    c = FOX_D * (n % 2) if fox else SWA_D * ((n - FOX_H) // 8)
                    v = (n // 2) % 2 if fox else FOX_PAIRS % 2
                    o = lambda t: ps[:, head_bank(n), t * dh:(t + 1) * dh]
                    pe.matmul(o(0), pT[:, n % 4, 0, :], vt[:, v, 0, c:c + dh], start=True, stop=True)
                    pe.matmul(o(1), pT[:, n % 4, 1, :], vt[:, v, 0, c:c + dh], start=True, stop=False)
                    pe.matmul(o(1), pT[:, n % 4, 2, :], vt[:, v, 1, c:c + dh], start=False, stop=True).then_inc(p_pv, 1)
                elif kind == "OT":
                    pe.wait_ge(v_on, n + 1)
                    for t in range(TT):
                        last = pe.transpose(ps[:, head_bank(n), T + t * P:T + (t + 1) * P], on[:, on_slot(n), t, :], ident[:, :])
                    last.then_inc(p_ot, 1)

            def scores(n):
                b = head_bank(n)
                if n < FOX_H:
                    pair = n // 2
                    pe.wait_ge(v_qn, 2 * pair + 2)
                    pe.wait_ge(v_c, 1)
                    pe.wait_ge(a_cst, 1)
                    if n >= 2:
                        pe.wait_ge(v_ol, n - 1)
                    q, k = qn[:, pair % 2, n % 2, :], kn[:, pair % 2, n % 2, :]
                    for t in range(TT):
                        keys = (t + 1) * P
                        o = ps[:, b, P * t:P * t + keys]
                        pe.matmul(o, q[:, t * P:(t + 1) * P], k[:, 0:keys], start=True, stop=False)
                        sel = ident[96:128, 112 + n:113 + n].to_broadcast([32, P])
                        pe.matmul(o, sel, nc_k[96:128, 0:keys], start=False, stop=False)
                        last = pe.matmul(ps[:, b, P * t + keys - P:P * t + keys], ident_r[:, :], mask_r[:, 0:P],
                                         start=False, stop=True)
                else:
                    h = n - FOX_H
                    m = h // 4 + 1
                    pe.wait_ge(v_qr, m + 1)
                    pe.wait_ge(a_kd, 1)
                    pe.wait_ge(a_cst, 2)
                    if h >= 4:
                        pe.wait_ge(v_ol, out_tile(n - 4)[0] + n % 2)
                        pe.wait_ge(v_on, n - 3)
                    else:
                        pe.wait_ge(v_ol, FOX_H)
                        pe.wait_ge(a_v, FOX_PAIRS + 1)
                    half = slice(SWA_D * (h % 2), SWA_D * (h % 2) + SWA_D)
                    q, k = qn[half, m % 2, h % 4 // 2, :], kdup[half, h // 8, :]
                    for t, (o0, k0, keys) in enumerate(((0, 0, P), (P, CHUNK, P + CHUNK))):
                        o = ps[:, b, o0:o0 + keys]
                        pe.matmul(o, q[:, t * P:(t + 1) * P], k[:, k0:k0 + keys], start=True, stop=False)
                        last = pe.matmul(o, ident_r[:, :], mask_r[:, o0:o0 + keys], start=False, stop=True)
                last.then_inc(p_s, 1)

            def mean_square(n):
                pe.wait_ge(v_ss, 8 * (n + 1))
                pe.matmul(ps[:, 0, 0:T], mean_d[:, :], ssacc[:, 0, :], start=True, stop=False)
                pe.matmul(ps[:, 0, 0:T], mean_d[:, :], ssacc[:, 1, :], start=False, stop=True).then_inc(p_ss, 1)

            def ffn(layer):
                base, it0, n0 = U_FFN[layer], UP_GROUPS * layer, KT * (2 * layer + 1)
                pe.wait_ge(a_r, 2 * layer + 2)
                pe.wait_ge(v_x, (X_OUT1 if layer else X_OUT0) + 8)
                with pe.Fori(0, UP_GROUPS) as i:
                    for j in range(16):
                        b = 4 * (j // 8)
                        if j == 0:
                            pe.wait_ge(v_gate, i + (it0 + 1))
                        if j == 8:
                            pe.wait_ge(v_up, i + (it0 + 1))
                        pe.wait_ge(lo_ready, 16 * i + (base + j + 1))
                        slot = (base + j) % RAW
                        for kj in range(2):
                            k = 2 * (j % 8) + kj
                            if j < 8:
                                pe.wait_ge(v_hl, n0 + k + 1)
                            for f in range(4):
                                last = mm_w(slot, kj, f, 4, hs[:, k, :, :], b + f, k == 0, k == KT - 1)
                        last.then_inc(unit_done, 1)
                base += 16 * UP_GROUPS
                xb = X_DOWN1 if layer else X_DOWN0
                pe.wait_ge(v_gate, it0 + UP_GROUPS + 1)
                with pe.Fori(0, 2) as i:
                    for j in range(2 * DOWN_UNITS):
                        g = j // DOWN_UNITS
                        if j % DOWN_UNITS == 0:
                            pe.wait_ge(v_up, it0 + UP_GROUPS + 1)
                            pe.wait_ge(v_x, 4 * i + (xb + 2 * g - 2))
                        pe.wait_ge(lo_ready, 2 * DOWN_UNITS * i + (base + j + 1))
                        slot = (base + j) % RAW
                        for kj in range(2):
                            k = 2 * (j % DOWN_UNITS) + kj
                            if g == 0:
                                pe.wait_ge(v_glo, it0 + k // 4 + 2)
                            for f in range(4):
                                last = mm_w(slot, kj, f, 4, gs[:, k // 4, k % 4, :, :], 4 * g + f, k == 0, k == FT - 1)
                        last.then_inc(unit_done, 1)

            pe.wait_ge(c_land, 8 * 16)
            for n in range(2 * LAYERS):
                last = pe.transpose(ps[:, 7, n * KT:(n + 1) * KT], grow[:, n, :], ident[0:KT, 0:KT])
            for n in range(4 * LAYERS):
                last = pe.transpose(ps[:, 6, n * FT:(n + 1) * FT], small[:, n, :], ident[0:FT, 0:FT])
            last.then_inc(p_tab, 1)
            for t in range(TT):
                pe.wait_ge(x_land[t], 16)
            for n in range(8):
                if n == 6:
                    pe.wait_ge(v_tab, 2)
                for k in range(2):
                    for t in range(TT):
                        f = 2 * n + k
                        last = pe.transpose(ps[:, n, k * T + t * P:k * T + (t + 1) * P], xin[:, t, f * P:(f + 1) * P], ident[:, :])
                last.then_inc(p_x, 1)
            mean_square(0)
            for s in fox_plan():
                step(s)
            for s in out_plan(U_FOX_OUT):
                step(s)
            mean_square(1)
            ffn(0)
            mean_square(2)
            for s in swa_plan() + out_plan(U_SWA_OUT):
                step(s)
            mean_square(3)
            ffn(1)
            for n in range(8):
                q, t = n // 2, n % 2
                if n == 0:
                    pe.wait_ge(v_x, X_DOWN1 + 8)
                for k in range(4):
                    last = pe.transpose(ps[:, n, k * P:(k + 1) * P], xT[:, 4 * q + k, t * P:(t + 1) * P], ident[:, :])
                last.then_inc(p_out, 1)


_INS = ["x", "attn_norm", "ffn_norm", "fox_w_in", "fox_f_bias", "fox_q_norm", "fox_k_norm", "fox_w_out",
        "swa_w_in", "swa_q_norm", "swa_k_norm", "swa_sinks", "swa_w_out", "ffn_w_up", "ffn_conv_w",
        "ffn_conv_b", "ffn_w_down"]


def kernel(**inputs):
    import concourse.bacc as bacc
    from concourse.bass_utils import run_bass_kernel_spmd

    nc = bacc.Bacc("TRN2", target_bir_lowering=False, num_devices=1)
    arrays, args = {}, []
    for name in _INS:
        a = np.ascontiguousarray(inputs[name])
        arrays[f"in_{name}"] = a
        args.append(nc.dram_tensor(f"in_{name}", a.shape, mybir.dt.from_np(a.dtype), kind="ExternalInput").ap())
    args.append(nc.dram_tensor("out_x", (1, T, D), F32, kind="ExternalOutput").ap())
    trunk(nc, *args)
    r = run_bass_kernel_spmd(nc, [arrays], core_ids=[0])
    return r.results[0]["out_x"]
```

```python
from contextlib import ExitStack

import numpy as np

import concourse.bass as bass
from concourse import mybir

F32 = mybir.dt.float32
F32R = mybir.dt.float32r
ACT = mybir.ActivationFunctionType
ALU = mybir.AluOpType
AX_X = mybir.AxisListType.X

P = 128
D = 2048
T = 256
TT = T // P
KT = D // P
FF = 11 * D // 4
FT = FF // P
LAYERS = 2
EPS = 1e-6

FOX_H, FOX_D = 16, 128
FOX_PAIRS = FOX_H // 2
SWA_H, SWA_KV, SWA_D = 32, 4, 64
SWA_GROUPS = SWA_H // 4
CHUNK = 64
NEG = -1e30

RAW = 4
UNIT = 1024
GROUP4 = 8
DOWN_UNITS = FT // 2
UP_GROUPS = FF // 512

U_F = 0
U_FOX = U_F + 2
U_FOX_OUT = U_FOX + 12 * FOX_PAIRS
U_FFN = [U_FOX_OUT + 32, 0]
U_SWA = U_FFN[0] + 2 * GROUP4 * UP_GROUPS + 4 * DOWN_UNITS
U_SWA_OUT = U_SWA + 8 + 4 * SWA_GROUPS
U_FFN[1] = U_SWA_OUT + 32
U_END = U_FFN[1] + 2 * GROUP4 * UP_GROUPS + 4 * DOWN_UNITS


def constant_table():
    i = np.arange(P)
    parts = {}
    parts["ident"] = np.eye(P)
    parts["mean_d"] = np.full((P, P), 1.0 / D)
    parts["mean_fox"] = np.full((P, P), 1.0 / FOX_D)
    parts["causal"] = np.where(i[:, None] >= i[None, :], 0.0, NEG)
    parts["mean_swa"] = (i[:, None] // SWA_D == i[None, :] // SWA_D) / SWA_D
    half = SWA_D // 2
    src = np.where(i % SWA_D < half, i + half, i - half)
    parts["swap"] = (i[:, None] == src[None, :]).astype(np.float64)
    inv = np.float32(10000.0) ** (-np.arange(half, dtype=np.float32) / np.float32(half))
    ang = np.arange(T, dtype=np.float32)[None, :] * inv.astype(np.float32)[i % half][:, None]
    parts["cos"] = np.cos(ang)
    parts["sin"] = np.sin(ang) * np.where(i % SWA_D < half, -1.0, 1.0)[:, None]
    qc = i // CHUNK
    k0 = np.arange(P) // CHUNK
    k1 = (CHUNK + np.arange(P + CHUNK)) // CHUNK
    sees = lambda q, k: np.where((k[None, :] <= q[:, None]) & (k[None, :] >= q[:, None] - 1), 0.0, NEG)
    parts["window0"] = sees(qc, k0)
    parts["window1"] = sees(qc + 2, k1)
    at, cols = {}, 0
    for name, a in parts.items():
        at[name] = (cols, cols + a.shape[1])
        cols += a.shape[1]
    return np.concatenate([a.astype(np.float32) for a in parts.values()], axis=1), at


def trunk(nc, x, attn_norm, ffn_norm, fox_w_in, fox_f_bias, fox_q_norm, fox_k_norm, fox_w_out,
          swa_w_in, swa_q_norm, swa_k_norm, swa_sinks, swa_w_out, ffn_w_up, ffn_conv_w,
          ffn_conv_b, ffn_w_down, out):
    table, col = constant_table()
    consts = nc.inline_tensor(table, name="const_table").ap()

    with ExitStack() as ctx:
        def sem(name):
            return ctx.enter_context(nc.semaphore(name))

        place = [nc.sbuf_base + (-nc.sbuf_base) % 64]

        def sb(name, shape, dt=F32, at=None):
            size = int(np.prod(shape[1:])) * 4
            size += -size % 32
            if at is None:
                at = place[0]
                place[0] += size
            assert at + size <= nc.sbuf_usable_end, (name, at + size)
            return nc.alloc_sbuf_tensor_at(name, shape, dt, offset=at)

        xT = sb("xT", [P, KT, T])
        hs = sb("hs", [P, KT, 2, T], F32R)
        raw = [sb(f"raw{s}", [P, UNIT]) for s in range(RAW)]
        whi = [sb(f"whi{s}", [P, UNIT], F32R) for s in range(RAW)]
        wlo = [sb(f"wlo{s}", [P, UNIT], F32R) for s in range(RAW)]
        ident = sb("ident", [P, P])
        mean_d = sb("mean_d", [P, P])
        gains = sb("gains", [P, 2 * LAYERS, KT])
        conv = sb("conv", [P, LAYERS, 4, FT])
        eps = sb("eps", [P, 1])
        rln = sb("rln", [P, T])
        rbc = sb("rbc", [P, T])
        rcol = sb("rcol", [P, TT])
        hf_at = place[0]
        hf = sb("hf", [P, 4, T])
        sqt = sb("sqt", [P, 2, 2, T])
        ssacc = sb("ssacc", [P, 2, T])
        gbuf = sb("gbuf", [P, 4, T + 2])
        ybuf_at = place[0]
        ybuf = sb("ybuf", [P, 4, T])
        region = place[0]
        xin = sb("xin", [P, TT, D], at=region)
        gs = sb("gs", [P, UP_GROUPS, 4, 2, T], F32R, at=region)
        inr = [region]

        def rg(name, shape, dt=F32):
            size = int(np.prod(shape[1:])) * 4
            size += -size % 32
            inr[0] += size
            assert inr[0] <= region + FT * 2 * T * 4
            return sb(name, shape, dt, at=inr[0] - size)

        oT = rg("oT", [P, KT, 2, T], F32R)
        qs = rg("qs", [P, 2, T])
        sq = rg("sq", [P, 2, T])
        lnb = rg("lnb", [P, 2, T])
        rb = rg("rb", [P, 2, T])
        qn = rg("qn", [P, 2, 2, T])
        kn = rg("kn", [P, 2, 2, T])
        tq = rg("tq", [P, 2, T])
        t1 = rg("t1", [P, 2, T])
        t2 = rg("t2", [P, 2, T])
        kdup = rg("kdup", [P, SWA_KV, T])
        vt = rg("vt", [P, 2, TT, T])
        pr = rg("pr", [P, 4, 3, P])
        pT = rg("pT", [P, 4, 3, P])
        on = rg("on", [P, 2, TT, P])
        mean_h = rg("mean_h", [P, P])
        swap = rg("swap", [P, P])
        cos = rg("cos", [P, T])
        sin = rg("sin", [P, T])
        mask = rg("mask", [P, 320])
        mask_r = rg("mask_r", [P, 320], F32R)
        ident_r = rg("ident_r", [P, P], F32R)
        nc_k = rg("nc_k", [P, T])
        fz = rg("fz", [P, T])
        fe = rg("fe", [P, T])
        fm = rg("fm", [P, T])
        ones_t = rg("ones_t", [P, T])
        mx = rg("mx", [P, 4, 2])
        nm = rg("nm", [P, 4, 2])
        es = rg("es", [P, 4, 2])
        ls = rg("ls", [P, 4, 2])
        rl = rg("rl", [P, 4, 2])
        qg = rg("qg", [P, 1])
        kg = rg("kg", [P, 1])
        qg0 = rg("qg0", [P, 1])
        fb = rg("fb", [P, 1])
        sinks = rg("sinks", [P, SWA_H])
        small = sb("small", [FT, 4 * LAYERS, P], at=ybuf_at)
        grow = sb("grow", [KT, 2 * LAYERS, P], at=hf_at)

        ps = ctx.enter_context(nc.psum_tensor("ps", [P, 8, 512], F32))

        w_land = [sem(f"w_land{s}") for s in range(RAW)]
        x_land = [sem(f"x_land{q}") for q in range(4)]
        i_land = sem("i_land")
        c_land = sem("c_land")
        f_land = sem("f_land")
        s_land = sem("s_land")
        o_land = sem("o_land")
        hi_ready = sem("hi_ready")
        lo_ready = sem("lo_ready")
        unit_done = sem("unit_done")
        v_set = sem("v_set")
        p_tab = sem("p_tab")
        v_tab = sem("v_tab")
        p_x = sem("p_x")
        v_x = sem("v_x")
        a_sqx = sem("a_sqx")
        v_ss = sem("v_ss")
        p_ss = sem("p_ss")
        a_rln = sem("a_rln")
        a_r = sem("a_r")
        p_rc = sem("p_rc")
        a_rc = sem("a_rc")
        a_hh = sem("a_hh")
        v_hl = sem("v_hl")
        v_x1 = sem("v_x1")
        a_fz = sem("a_fz")
        v_f = sem("v_f")
        a_f = sem("a_f")
        v_c = sem("v_c")
        a_cst = sem("a_cst")
        v_gain = sem("v_gain")
        a_half = sem("a_half")
        v_q1 = sem("v_q1")
        v_qs = sem("v_qs")
        a_sq = sem("a_sq")
        p_ssq = sem("p_ssq")
        a_ln = sem("a_ln")
        a_rk = sem("a_rk")
        v_qn = sem("v_qn")
        p_rot = sem("p_rot")
        v_rope = sem("v_rope")
        v_qr = sem("v_qr")
        a_kd = sem("a_kd")
        a_v = sem("a_v")
        p_s = sem("p_s")
        v_mx = sem("v_mx")
        v_nm = sem("v_nm")
        a_ex = sem("a_ex")
        v_l = sem("v_l")
        v_rl = sem("v_rl")
        p_pt = sem("p_pt")
        a_pt = sem("a_pt")
        p_pv = sem("p_pv")
        v_on = sem("v_on")
        p_ot = sem("p_ot")
        a_oh = sem("a_oh")
        v_ol = sem("v_ol")
        a_g = sem("a_g")
        v_gate = sem("v_gate")
        v_gr = sem("v_gr")
        v_yr = sem("v_yr")
        v_tap = sem("v_tap")
        a_silu = sem("a_silu")
        a_u = sem("a_u")
        v_up = sem("v_up")
        v_gu = sem("v_gu")
        a_gh = sem("a_gh")
        v_glo = sem("v_glo")
        p_out = sem("p_out")
        v_out = sem("v_out")
        a_out = sem("a_out")

        def rows(w, k0, kk, c0, cc):
            return w[k0 * P:(k0 + kk) * P, c0:c0 + cc].rearrange("(k p) c -> p k c", p=P)

        fox_in, swa_in = fox_w_in[0], swa_w_in[0]
        fox_cols = [0, D, 2 * D]
        F0 = 3 * D + FOX_H - P

        OUT_EARLY = 6
        OUT_ORDER = list(enumerate([(g, j) for g in (0, 1) for j in range(3)] + [(0, 3), (1, 3)]
                                   + [(g, j) for g in range(2, 8) for j in range(4)]))

        def fox_plan():
            steps = [("unit", U_F, "f", 0, 0), ("unit", U_F + 1, "f", 0, 1)]
            outs = iter(OUT_ORDER[:OUT_EARLY])
            for p in range(FOX_PAIRS + 1):
                a, b = 2 * (p - 1), 2 * (p - 1) + 1
                old, new = p > 0, p < FOX_PAIRS
                for j in range(12):
                    q, k = 2 * p, 2 * p + 1
                    if old:
                        steps += {0: [("ex", a)], 1: [("ex", b)], 4: [("on", a)], 5: [("on", b)],
                                  7: [("oh", a)], 8: [("oh", b)]}.get(j, [])
                    if new:
                        steps += {3: [("evac", q)], 4: [("sq", q)], 6: [("qn", q)], 7: [("evac", k)], 8: [("sq", k)],
                                  10: [("qn", k)], 11: [("evac_v", p)]}.get(j, [])
                        steps.append(("unit", U_FOX + 12 * p + j, "qkv"[j // 4], p, j % 4))
                        if p == 0:
                            steps += {2: [("stats", 0)], 4: [("f", 0)], 6: [("rcol", 0)]}.get(j, [])
                        steps += {5: [("ssq", q)], 9: [("ssq", k)]}.get(j, [])
                    elif j % 4 != 3 and j < 7:
                        n, (g, i) = next(outs)
                        steps.append(("unit", U_FOX_OUT + n, "o", g, i))
                    if old:
                        steps += {0: [("S", b)], 1: [("PT", a)], 2: [("PT", b)], 3: [("PV", a)], 4: [("PV", b)],
                                  6: [("OT", a)], 7: [("OT", b)]}.get(j, [])
                    if new and j == 11:
                        steps.append(("S", 2 * p))
            return steps

        FOX_N = 2 * FOX_PAIRS

        def swa_plan():
            steps = [("unit", U_SWA + j, "k", 0, j) for j in range(3)] + [("stats", 2)]
            steps += [("unit", U_SWA + 3, "k", 0, 3), ("evac", FOX_N), ("unit", U_SWA + 4, "v", 0, 0), ("rcol", 2),
                      ("sq", FOX_N), ("unit", U_SWA + 5, "v", 0, 1), ("ssq", FOX_N), ("unit", U_SWA + 6, "v", 0, 2),
                      ("qn", FOX_N), ("unit", U_SWA + 7, "v", 0, 3), ("evac_v", FOX_PAIRS), ("rot", FOX_N)]
            chain = {4: ["sq"], 5: ["ssq"], 6: ["qn"], 7: ["rot"], 8: ["S0"], 9: ["ex0", "S1"],
                     10: ["ex1", "PT0", "S2"], 11: ["ex2", "PV0", "PT1", "S3"], 12: ["on0", "ex3", "PV1", "PT2"],
                     13: ["on1", "PV2", "PT3"], 14: ["on2", "OT1", "PV3"], 15: ["oh1", "on3"], 16: ["OT3"], 17: ["oh3"]}
            before, after = ("oh", "on", "qn", "sq", "ex"), ("OT", "ssq", "rot", "PV", "PT", "S")

            def steps_of(slot, kinds):
                return [(kind, FOX_N + 1 + g if kind in ("sq", "ssq", "qn", "rot") else FOX_H + 4 * g + int(what[-1]))
                        for kind in kinds for g in range(SWA_GROUPS) for what in chain.get(slot - 4 * g, [])
                        if what.rstrip("0123") == kind]

            for slot in range(4 * (SWA_GROUPS - 1) + 18):
                i = slot // 4
                steps += steps_of(slot, before)
                if i < SWA_GROUPS:
                    if slot % 4 == 3:
                        steps.append(("evac", FOX_N + 1 + i))
                    steps.append(("unit", U_SWA + 8 + slot, "q", i, slot % 4))
                elif slot - 4 * SWA_GROUPS in (1, 5, 8):
                    n = (1, 5, 8).index(slot - 4 * SWA_GROUPS)
                    steps.append(("unit", U_SWA_OUT + n, "o", 0, n))
                steps += steps_of(slot, after)
            return steps

        def out_plan(base):
            if base == U_FOX_OUT:
                return [("unit", base + n, "o", g, j) for n, (g, j) in OUT_ORDER[OUT_EARLY:]]
            return [("unit", base + n, "o", n // 4, n % 4) for n in range(3, 32)]

        def head_bank(h):
            return 4 + h % 2 if h < FOX_H else 2 + h % 4

        def out_bank(h):
            return head_bank(h) if h < FOX_H else 7

        def stats_bank(n):
            return (5, 7, 6, 7)[n]

        def proj_banks(u):
            if u < U_FOX:
                return 6
            if u < U_FOX_OUT:
                return 2 * ((u - U_FOX) // 4 % 2)
            if u < U_FFN[0]:
                return 2 * (OUT_ORDER[u - U_FOX_OUT][1][0] % 2)
            if u < U_SWA_OUT:
                if U_SWA + 12 <= u < U_SWA + 16:
                    return 4
                return 0 if u >= U_SWA + 8 or u < U_SWA + 4 else 3
            return 2 * ((u - U_SWA_OUT) // 4 % 2)

        def norm_last(n):
            if n < FOX_N:
                return U_FOX + 12 * (n // 2) + 4 * (n % 2) + 3
            return U_SWA + 3 if n == FOX_N else U_SWA + 8 + 4 * (n - FOX_N - 1) + 3

        def norm_bank(n):
            return proj_banks(norm_last(n))

        def v_last(n):
            return U_FOX + 12 * n + 11 if n < FOX_PAIRS else U_SWA + 7

        def out_tile(h):
            if h < FOX_H:
                return h, h
            return FOX_H + (h - FOX_H) // 2, (h - FOX_H) // 2

        def on_slot(h):
            return out_tile(h)[0] % 2

        def x_pair(i, h):
            return xT[:, :, :].rearrange("p (i h k) t -> p i h k t", i=2, h=4)[:, i, h, :, :]

        GAIN = (0, 2, 1, 3)

        def down_tile(i, g, q):
            split = "p (i g q) -> p i g q"
            return (xT[:, :, :].rearrange("p (i g q) t -> p i g q t", i=2, g=2)[:, i, g, q, :],
                    gains[:, GAIN[2], :].rearrange(split, i=2, g=2)[:, i, g, q:q + 1],
                    hs[:, :, :, :].rearrange("p (i g q) h t -> p i g q h t", i=2, g=2)[:, i, g, q, :, :])

        X_LOAD, X_OUT0, X_DOWN0, X_OUT1, X_DOWN1 = (8 * n for n in range(5))

        block = ctx.enter_context(nc.Block())

        @block.sync
        def _(sp):
            for q in range(4):
                for t in range(TT):
                    c = slice(512 * q, 512 * q + 512)
                    sp.dma_start(xin[:, t, c], x[0, t * P:(t + 1) * P, c]).then_inc(x_land[q], 16)

            def load(u, src, slot):
                n = src.shape[1]
                if not isinstance(u, int) or u >= RAW:
                    sp.wait_ge(lo_ready, u - RAW + 1)
                sp.dma_start(raw[slot][:, :].rearrange("p (k c) -> p k c", k=n), src)\
                    .then_inc(w_land[slot], 16)

            for j in range(2):
                load(U_F + j, rows(fox_in, 8 * j, 8, F0, P), (U_F + j) % RAW)
            cs = lambda name: consts[:, col[name][0]:col[name][1]]
            for p in range(FOX_PAIRS):
                for j in range(12):
                    u = U_FOX + 12 * p + j
                    if u == RAW:
                        for dst, src in ((mean_d[:, :], cs("mean_d")), (mean_h[:, :], cs("mean_fox")),
                                         (mask[:, 0:P], cs("causal")),
                                         (qg0[:, :], fox_q_norm[0].rearrange("(p a) -> p a", a=1)),
                                         (kg[:, :], fox_k_norm[0].rearrange("(p a) -> p a", a=1))):
                            sp.dma_start(dst, src).then_inc(f_land, 16)
                        sp.wait_ge(v_set, 4)
                        sp.dma_start(fb[112:128, :], fox_f_bias[0].rearrange("(p a) -> p a", a=1)).then_inc(f_land, 16)
                    load(u, rows(fox_in, 4 * (j % 4), 4, fox_cols[j // 4] + 256 * p, 256), u % RAW)
            for n, (g, j) in OUT_ORDER:
                load(U_FOX_OUT + n, rows(fox_w_out[0], 4 * j, 4, 256 * g, 256), (U_FOX_OUT + n) % RAW)

            def ffn_loads(layer):
                base = U_FFN[layer]
                with sp.Fori(0, UP_GROUPS) as i:
                    for j in range(16):
                        w = ffn_w_up[layer].rearrange("(k p) (h g c) -> p k h g c", p=P, h=2, c=512)
                        k0 = 2 * (j % 8)
                        load(base + 16 * i + j, w[:, k0:k0 + 2, j // 8, i, :], (base + j) % RAW)
                base += 16 * UP_GROUPS
                with sp.Fori(0, 2) as i:
                    for j in range(2 * DOWN_UNITS):
                        w = ffn_w_down[layer].rearrange("(k p) (i g c) -> p k i g c", p=P, i=2, c=512)
                        k0 = 2 * (j % DOWN_UNITS)
                        load(base + 2 * DOWN_UNITS * i + j, w[:, k0:k0 + 2, i, j // DOWN_UNITS, :],
                             (base + j) % RAW)

            ffn_loads(0)
            for j in range(8):
                load(U_SWA + j, rows(swa_in, 4 * (j % 4), 4, D + 256 * (j // 4), 256), (U_SWA + j) % RAW)
            small_loads = [(t, cs(name)) for t, name in
                           ((mean_h[:, :], "mean_swa"), (mask[:, 0:P], "window0"), (mask[:, P:320], "window1"),
                            (swap[:, :], "swap"), (cos[:, :], "cos"), (sin[:, :], "sin"))]
            for half in range(2):
                sl = slice(SWA_D * half, SWA_D * half + SWA_D)
                small_loads.append((qg0[sl, :], swa_q_norm[0].rearrange("(p a) -> p a", a=1)))
                small_loads.append((kg[sl, :], swa_k_norm[0].rearrange("(p a) -> p a", a=1)))
            small_loads.append((sinks[:, :], swa_sinks[0].partition_broadcast(P)))
            sp.wait_ge(unit_done, U_SWA)
            for n in range(4 * SWA_GROUPS):
                for dst, src in small_loads[4 * n:4 * n + 4]:
                    sp.dma_start(dst, src).then_inc(s_land, 16)
                u = U_SWA + 8 + n
                load(u, rows(swa_in, 4 * (n % 4), 4, 256 * (n // 4), 256), u % RAW)
            for n in range(32):
                load(U_SWA_OUT + n, rows(swa_w_out[0], 4 * (n % 4), 4, 256 * (n // 4), 256), (U_SWA_OUT + n) % RAW)
            ffn_loads(1)
            for n in range(8):
                q, t = n // 2, n % 2
                sp.wait_ge(a_out if t else v_out, q + 1)
                sp.dma_start(out[0, t * P:(t + 1) * P, 512 * q:512 * q + 512],
                             xin[:, t, 512 * q:512 * q + 512]).then_inc(o_land, 16)
            sp.wait_ge(o_land, 8 * 16)

        @block.scalar
        def _(act):
            cs = lambda name: consts[:, col[name][0]:col[name][1]]
            act.preload_act_table_set("natural_log_exp_and_others")
            act.dma_start(ident[:, :], cs("ident")).then_inc(i_land, 16)
            for n, g in enumerate((attn_norm, ffn_norm)):
                act.dma_start(grow[:, 2 * n:2 * n + 2, :], g.rearrange("l (k p) -> k l p", p=P)).then_inc(c_land, 16)
            for l in range(LAYERS):
                act.dma_start(small[:, 4 * l:4 * l + 3, :],
                              ffn_conv_w[l].rearrange("j (f p) -> f j p", p=P)).then_inc(c_land, 16)
                act.dma_start(small[:, 4 * l + 3, :], ffn_conv_b[l].rearrange("(f p) -> f p", p=P)).then_inc(c_land, 16)

            def conv_hi(u, slot):
                act.wait_ge(w_land[slot], 16 * (u // RAW + 1))
                if u >= RAW:
                    act.wait_ge(unit_done, u - RAW + 1)
                act.activation(whi[slot][:, :], raw[slot][:, :], ACT.Copy).then_inc(hi_ready, 1)

            def conv_hi_loop(first, step, i, j):
                u0 = first + j
                act.wait_ge(w_land[u0 % RAW], (step // RAW * 16) * i + 16 * (u0 // RAW + 1))
                act.wait_ge(unit_done, step * i + (u0 - RAW + 1))
                act.activation(whi[u0 % RAW][:, :], raw[u0 % RAW][:, :], ACT.Copy).then_inc(hi_ready, 1)

            def square_x(n, pair):
                act.wait_ge(v_x, n + 1)
                if n >= 2:
                    act.wait_ge(v_ss, n - 1)
                act.activation(sqt[:, n % 2, :, :], xT[:, 2 * pair:2 * pair + 2, :], ACT.Square).then_inc(a_sqx, 1)

            def prep_hi(n, k, x_tile, gain, h_tile):
                act.activation(h_tile[:, 0, :], x_tile, ACT.Copy, scale=gain).then_inc(a_hh, 1)

            def prep(n, pair):
                for k in (2 * pair, 2 * pair + 1):
                    prep_hi(n, k, xT[:, k, :], gains[:, GAIN[n], k:k + 1], hs[:, k, :, :])

            def stats(n):
                b = stats_bank(n)
                act.wait_ge(p_ss, n + 1)
                act.activation(rln[:, :], ps[:, b, 0:T], ACT.Ln, bias=eps[:, 0:1]).then_inc(a_rln, 1)
                act.wait_ge(a_rln, n + 1)
                act.activation(rbc[:, :], rln[:, :], ACT.Exp, scale=-0.5).then_inc(a_r, 1)

            def step(s):
                kind, n = s[0], s[1]
                if kind == "unit":
                    if n + RAW < U_END:
                        conv_hi(n + RAW, (n + RAW) % RAW)
                    if s[2] == "o" and s[4] == 3:
                        square_x(X_OUT0 + s[3] if n < U_FFN[0] else X_OUT1 + s[3], s[3])
                        prep(1 if n < U_FFN[0] else 3, s[3])
                elif kind == "stats":
                    stats(n)
                elif kind == "rcol":
                    act.wait_ge(p_rc, n // 2 + 1)
                    act.activation(rcol[:, :], ps[:, stats_bank(n), T:T + TT], ACT.Copy).then_inc(a_rc, 1)
                elif kind == "f":
                    act.wait_ge(unit_done, U_FOX)
                    act.wait_ge(f_land, 6 * 16)
                    act.activation(fz[96:128, :], ps[96:128, 6, 0:T], ACT.Copy).then_inc(a_fz, 1)
                    act.wait_ge(v_f, 6)
                    act.activation(fe[96:128, :], fm[96:128, :], ACT.Exp, scale=-1.0).then_inc(a_f, 1)
                    act.wait_ge(a_f, 1)
                    act.activation(fe[96:128, :], fe[96:128, :], ACT.Ln, bias=ones_t[96:128, 0:1]).then_inc(a_f, 1)
                    act.activation(mask_r[:, 0:P], mask[:, 0:P], ACT.Copy)
                    act.activation(ident_r[:, :], ident[:, :], ACT.Copy).then_inc(a_cst, 1)
                elif kind == "evac":
                    b = norm_bank(n)
                    act.wait_ge(unit_done, norm_last(n) + 1)
                    if n > 0:
                        act.wait_ge(v_qn, n)
                    act.activation(qs[:, :, :], ps[:, b:b + 2, 0:T], ACT.Copy).then_inc(a_half, 1)
                elif kind == "sq":
                    act.wait_ge(v_qs, n + 1)
                    act.activation(sq[:, :, :], qs[:, :, :], ACT.Square).then_inc(a_sq, 1)
                elif kind == "ssq":
                    if n == FOX_N + 1:
                        act.wait_ge(v_qr, 1)
                        for kv in range(SWA_KV):
                            lo = SWA_D * (kv % 2)
                            src = qn[lo:lo + SWA_D, 0, kv // 2, :]
                            act.activation(kdup[0:SWA_D, kv, :], src, ACT.Copy)
                            last = act.activation(kdup[SWA_D:P, kv, :], src, ACT.Copy)
                        last.then_inc(a_kd, 1)
                    act.wait_ge(p_ssq, n + 1)
                    act.activation(lnb[:, :, :], ps[:, 7, :].rearrange("p (f t) -> p f t", f=2), ACT.Ln,
                                   bias=eps[:, 0:1]).then_inc(a_ln, 1)
                    act.wait_ge(a_ln, n + 1)
                    act.activation(rb[:, :, :], lnb[:, :, :], ACT.Exp, scale=-0.5).then_inc(a_rk, 1)
                elif kind == "evac_v":
                    act.wait_ge(unit_done, v_last(n) + 1)
                    if n >= 2:
                        act.wait_ge(p_pv, 2 * (n - 1))
                    b = proj_banks(v_last(n))
                    act.wait_ge(a_rc, 1 if n < FOX_PAIRS else 2)
                    for t in range(TT):
                        last = act.activation(vt[:, n % 2, t, :], ps[:, b, T * t:T * (t + 1)], ACT.Copy,
                                              scale=rcol[:, t:t + 1])
                    last.then_inc(a_v, 1)
                elif kind == "ex":
                    act.wait_ge(v_nm, n + 1)
                    if n >= 4:
                        act.wait_ge(p_pt, n - 3)
                    r, b = n % 4, head_bank(n)
                    act.activation(pr[:, r, 0, :], ps[:, b, 0:P], ACT.Exp, bias=nm[:, r, 0:1],
                                   accum_out=ls[:, r, 0:1])
                    if n < FOX_H:
                        last = act.activation(pr[:, r, 1:3, :], ps[:, b, P:3 * P].rearrange("p (a c) -> p a c", a=2),
                                              ACT.Exp, bias=nm[:, r, 1:2], accum_out=ls[:, r, 1:2])
                    else:
                        flat = pr[:, r, :, :].rearrange("p a c -> p (a c)")
                        act.wait_ge(v_set, 6)
                        act.activation(flat[:, P + CHUNK:3 * P], ps[:, b, P:P + 192], ACT.Exp,
                                       bias=nm[:, r, 1:2], accum_out=ls[:, r, 1:2])
                        last = act.activation(es[:, r, :], nm[:, r, :], ACT.Exp, bias=sinks[:, n - FOX_H:n - FOX_H + 1])
                    last.then_inc(a_ex, 1)
                elif kind == "PT":
                    act.wait_ge(p_pt, n + 1)
                    if n >= 4:
                        act.wait_ge(p_pv, n - 3)
                    act.activation(pT[:, n % 4, :, :], ps[:, 6, 0:3 * P].rearrange("p (a c) -> p a c", a=3),
                                   ACT.Copy).then_inc(a_pt, 1)
                elif kind == "oh":
                    j, k = out_tile(n)
                    act.wait_ge(p_ot, j + 1)
                    act.activation(oT[:, k, 0, :], ps[:, out_bank(n), T:2 * T], ACT.Copy).then_inc(a_oh, 1)

            def ffn(layer):
                base, it0 = U_FFN[layer], UP_GROUPS * layer

                def up_group(i, first):
                    for j in range(16):
                        conv_hi_loop(base + RAW, 16, i, j)
                        if first and j == 3:
                            stats(2 * layer + 1)
                            act.preload_act_table_set("silu_and_others")
                        if j == 7:
                            act.wait_ge(unit_done, 16 * i + (base + 8))
                            act.wait_ge(v_tap, 3 * i + (3 * it0 + 1))
                            act.activation(gbuf[:, :, 2:T + 2], ps[:, 0:4, 0:T], ACT.Copy).then_inc(a_g, 1)
                        if j == 11:
                            act.wait_ge(v_tap, 3 * i + (3 * it0 + 4))
                            act.activation(ybuf[:, :, :], ybuf[:, :, :], ACT.Silu).then_inc(a_silu, 1)
                        if j == 15:
                            act.wait_ge(unit_done, 16 * i + (base + 16))
                            act.wait_ge(v_glo, i + (it0 + 1))
                            act.activation(hf[:, :, :], ps[:, 4:8, 0:T], ACT.Copy).then_inc(a_u, 1)
                            act.wait_ge(v_gu, i + (it0 + 1))
                            act.activation(gs[:, i, :, 0, :], hf[:, :, :], ACT.Copy).then_inc(a_gh, 1)

                up_group(0, True)
                with act.Fori(1, UP_GROUPS) as i:
                    up_group(i, False)
                act.preload_act_table_set("natural_log_exp_and_others")
                base += 16 * UP_GROUPS
                xb = X_DOWN1 if layer else X_DOWN0
                if layer == 0:
                    with act.Fori(0, 2) as i:
                        for j in range(2 * DOWN_UNITS):
                            conv_hi_loop(base + RAW, 2 * DOWN_UNITS, i, j)
                            if j % DOWN_UNITS == DOWN_UNITS - 1:
                                for h in range(2):
                                    n = xb + 2 * (j // DOWN_UNITS) + h
                                    act.wait_ge(v_x, 4 * i + (n + 1))
                                    act.wait_ge(v_ss, 4 * i + (n - 1))
                                    act.activation(sqt[:, n % 2, :, :], x_pair(i, 2 * (j // DOWN_UNITS) + h),
                                                   ACT.Square).then_inc(a_sqx, 1)
                                for q in range(4):
                                    x_tile, gain, h_tile = down_tile(i, j // DOWN_UNITS, q)
                                    prep_hi(2, None, x_tile, gain, h_tile)
                else:
                    for u in range(base, U_END - RAW):
                        conv_hi(u + RAW, (u + RAW) % RAW)

            for n in range(3):
                square_x(X_LOAD + n, n)
            conv_hi(0, 0)
            conv_hi(1, 1)
            act.wait_ge(v_tab, 2)
            for n in range(8):
                act.wait_ge(v_x, n + 1)
                prep(0, n)
            for u in range(2, RAW):
                conv_hi(u, u)
            for n in range(3, 8):
                square_x(X_LOAD + n, n)
            for s in fox_plan() + out_plan(U_FOX_OUT):
                step(s)
            ffn(0)
            for s in swa_plan() + out_plan(U_SWA_OUT):
                if s == ("qn", FOX_N):
                    act.wait_ge(s_land, 11 * 16)
                    act.activation(mask_r[:, :], mask[:, :], ACT.Copy)
                    act.activation(ident_r[:, :], ident[:, :], ACT.Copy).then_inc(a_cst, 1)
                step(s)
            ffn(1)
            for n in range(1, 8, 2):
                act.wait_ge(p_out, n + 1)
                q = n // 2
                act.activation(xin[:, 1, 512 * q:512 * q + 512], ps[:, n, :], ACT.Copy).then_inc(a_out, 1)

        @block.vector
        def _(dve):
            tt = dve.tensor_tensor

            def conv_lo(u):
                slot = u % RAW
                dve.wait_ge(hi_ready, u + 1)
                tt(wlo[slot][:, :], raw[slot][:, :], whi[slot][:, :].bitcast(F32), ALU.subtract).then_inc(lo_ready, 1)

            def conv_lo_loop(first, step_, i, j):
                u0 = first + j
                slot = u0 % RAW
                dve.wait_ge(hi_ready, step_ * i + (u0 + 1))
                tt(wlo[slot][:, :], raw[slot][:, :], whi[slot][:, :].bitcast(F32), ALU.subtract).then_inc(lo_ready, 1)

            def add_square(n):
                dve.wait_ge(a_sqx, n + 1)
                if n % 8 == 0:
                    if n:
                        dve.wait_ge(p_ss, n // 8)
                    dve.tensor_copy(ssacc[:, :, :], sqt[:, n % 2, :, :]).then_inc(v_ss, 1)
                else:
                    dve.wait_ge(v_ss, n)
                    tt(ssacc[:, :, :], ssacc[:, :, :], sqt[:, n % 2, :, :], ALU.add).then_inc(v_ss, 1)

            def residual(n, n1, xs, b, wide):
                tt(xs, xs, ps[:, b:b + wide, 0:T], ALU.add).then_inc(v_x1, 1)
                dve.wait_ge(v_x1, n1)
                tt(xs, xs, ps[:, b:b + wide, T:2 * T], ALU.add).then_inc(v_x, wide // 2)

            def prep_lo(n, k, x_tile, gain, h_tile):
                dve.scalar_tensor_tensor(h_tile[:, 1, :], x_tile, gain, h_tile[:, 0, :].bitcast(F32),
                                         ALU.mult, ALU.subtract).then_inc(v_hl, 1)

            def prep(n, pair):
                for k in (2 * pair, 2 * pair + 1):
                    dve.wait_ge(a_hh, KT * n + k + 1)
                    prep_lo(n, k, xT[:, k, :], gains[:, GAIN[n], k:k + 1], hs[:, k, :, :])

            def step(s):
                kind, n = s[0], s[1]
                if kind == "unit":
                    xb, g = X_OUT0 if n < U_FFN[0] else X_OUT1, s[3]
                    last = s[2] == "o" and s[4] == 3
                    if last:
                        dve.wait_ge(unit_done, n + 1)
                        residual(xb + g, 1 + g + (12 if n >= U_FFN[0] else 0), xT[:, 2 * g:2 * g + 2, :], proj_banks(n), 2)
                    if n + RAW < U_END:
                        conv_lo(n + RAW)
                    if last:
                        add_square(xb + g)
                        prep(1 if n < U_FFN[0] else 3, g)
                elif kind == "f":
                    r = slice(96, 128)
                    dve.wait_ge(a_fz, 1)
                    tt(fz[r, :], fz[r, :], ps[r, 6, T:2 * T], ALU.add).then_inc(v_f, 1)
                    dve.wait_ge(v_f, 1)
                    dve.wait_ge(a_r, 1)
                    dve.wait_ge(f_land, 6 * 16)
                    tt(fz[r, :], fz[r, :], rbc[r, :], ALU.mult).then_inc(v_f, 1)
                    dve.wait_ge(v_f, 2)
                    dve.tensor_scalar(fz[r, :], fz[r, :], fb[r, 0:1], None, ALU.add).then_inc(v_f, 1)
                    dve.wait_ge(v_f, 3)
                    dve.memset(fz[96:112, :], 0.0).then_inc(v_f, 1)
                    dve.wait_ge(v_f, 4)
                    dve.tensor_scalar(fm[r, :], fz[r, :], -1.0, None, ALU.mult).then_inc(v_f, 1)
                    dve.wait_ge(v_f, 5)
                    tt(fm[r, :], fm[r, :], fz[r, :], ALU.max).then_inc(v_f, 1)
                    dve.wait_ge(v_f, 6)
                    dve.tensor_scalar(fz[r, :], fz[r, :], 0.0, None, ALU.min).then_inc(v_f, 1)
                    dve.wait_ge(v_f, 7)
                    dve.wait_ge(a_f, 2)
                    tt(fz[r, :], fe[r, :], fz[r, :], ALU.subtract).then_inc(v_f, 1)
                    dve.wait_ge(v_f, 8)
                    dve.tensor_tensor_scan(nc_k[r, :], ones_t[r, :], fz[r, :], 0.0, ALU.mult, ALU.add).then_inc(v_c, 1)
                    dve.tensor_scalar(qg[:, :], qg0[:, :], FOX_D ** -0.5, None, ALU.mult).then_inc(v_gain, 1)
                elif kind == "evac":
                    b = norm_bank(n)
                    dve.wait_ge(a_half, n + 1)
                    tt(qs[:, :, :], qs[:, :, :], ps[:, b:b + 2, T:2 * T], ALU.add).then_inc(v_q1, 1)
                    dve.wait_ge(v_q1, n + 1)
                    dve.wait_ge(a_r, 1 if n < FOX_N else 3)
                    tt(qs[:, :, :], qs[:, :, :], rbc[:, None, :].to_broadcast([P, 2, T]), ALU.mult).then_inc(v_qs, 1)
                elif kind == "qn":
                    dve.wait_ge(a_rk, n + 1)
                    dve.wait_ge(v_qs, n + 1)
                    if n == FOX_N:
                        dve.wait_ge(s_land, 11 * 16)
                        dve.tensor_scalar(qg[:, :], qg0[:, :], SWA_D ** -0.5, None, ALU.mult).then_inc(v_gain, 1)
                    dve.wait_ge(v_gain, 1 if n < FOX_N else 2)
                    if n < FOX_N:
                        pair = n // 2
                        if pair >= 2:
                            dve.wait_ge(p_s, 2 * (pair - 1))
                        dst = (kn if n % 2 else qn)[:, pair % 2, :, :]
                        g = kg if n % 2 else qg
                    else:
                        dst, g = tq[:, :, :], (kg if n == FOX_N else qg)
                        if n > FOX_N:
                            dve.wait_ge(p_rot, n - FOX_N)
                    dve.scalar_tensor_tensor(dst, qs[:, :, :], g[:, 0:1], rb[:, :, :], ALU.mult, ALU.mult).then_inc(v_qn, 1)
                elif kind == "rot":
                    m = n - FOX_N
                    dve.wait_ge(v_qn, n + 1)
                    if m:
                        dve.wait_ge(v_qr, m)
                    tt(t1[:, :, :], tq[:, :, :], cos[:, None, :].to_broadcast([P, 2, T]), ALU.mult)
                    dve.wait_ge(p_rot, m + 1)
                    tt(t2[:, :, :], ps[:, 7, :].rearrange("p (f t) -> p f t", f=2),
                       sin[:, None, :].to_broadcast([P, 2, T]), ALU.mult).then_inc(v_rope, 1)
                    dve.wait_ge(v_rope, m + 1)
                    if m == 2:
                        dve.wait_ge(a_kd, 1)
                    if m >= 3:
                        dve.wait_ge(p_s, FOX_H + 4 * (m - 2))
                    tt(qn[:, m % 2, :, :], t1[:, :, :], t2[:, :, :], ALU.add).then_inc(v_qr, 1)
                elif kind == "S":
                    r, b = n % 4, head_bank(n)
                    dve.wait_ge(p_s, n + 1)
                    dve.reduce_max(mx[:, r, 0:1], ps[:, b, 0:P], AX_X)
                    end = 3 * P if n < FOX_H else P + 192
                    dve.reduce_max(mx[:, r, 1:2], ps[:, b, P:end], AX_X).then_inc(v_mx, 1)
                    dve.wait_ge(v_mx, n + 1)
                    if n < FOX_H:
                        dve.tensor_scalar(nm[:, r, :], mx[:, r, :], -1.0, None, ALU.mult).then_inc(v_nm, 1)
                    else:
                        h = n - FOX_H
                        dve.tensor_scalar(nm[:, r, :], mx[:, r, :], sinks[:, h:h + 1], -1.0, ALU.max, ALU.mult).then_inc(v_nm, 1)
                elif kind == "PT":
                    r = n % 4
                    dve.wait_ge(a_ex, n + 1)
                    if n >= FOX_H:
                        tt(ls[:, r, :], ls[:, r, :], es[:, r, :], ALU.add).then_inc(v_l, 1)
                        dve.wait_ge(v_l, n - FOX_H + 1)
                    dve.reciprocal(rl[:, r, :], ls[:, r, :]).then_inc(v_rl, 1)
                elif kind == "on":
                    dve.wait_ge(p_pv, n + 1)
                    dve.wait_ge(v_rl, n + 1)
                    j = out_tile(n)[0]
                    if j >= 2:
                        dve.wait_ge(p_ot, j - 1)
                    dh = FOX_D if n < FOX_H else SWA_D
                    c = 0 if n < FOX_H else SWA_D * (n % 2)
                    for t in range(TT):
                        last = dve.tensor_scalar(on[:, on_slot(n), t, c:c + dh], ps[:, head_bank(n), t * dh:(t + 1) * dh],
                                                 rl[:, n % 4, t:t + 1], None, ALU.mult)
                    last.then_inc(v_on, 1)
                elif kind == "oh":
                    j, k = out_tile(n)
                    dve.wait_ge(a_oh, j + 1)
                    tt(oT[:, k, 1, :], ps[:, out_bank(n), T:2 * T], oT[:, k, 0, :].bitcast(F32),
                       ALU.subtract).then_inc(v_ol, 1)

            def ffn(layer):
                base, it0 = U_FFN[layer], UP_GROUPS * layer

                rms4 = rbc[:, None, :].to_broadcast([P, 4, T])

                def up_group(i):
                    for j in range(16):
                        conv_lo_loop(base + RAW, 16, i, j)
                        if j == 7:
                            dve.wait_ge(a_g, i + (it0 + 1))
                            tt(gbuf[:, :, 2:T + 2], gbuf[:, :, 2:T + 2], ps[:, 0:4, T:2 * T], ALU.add).then_inc(v_gate, 1)
                            dve.wait_ge(v_gate, i + (it0 + 2))
                            dve.wait_ge(a_r, 2 * layer + 2)
                            tt(gbuf[:, :, 2:T + 2], gbuf[:, :, 2:T + 2], rms4, ALU.mult).then_inc(v_gr, 1)
                            dve.wait_ge(v_gr, i + (it0 + 1))
                            taps = conv[:, layer, :, :].rearrange("p w (i f) -> p w i f", f=4)
                        if 7 <= j < 10:
                            w = j - 7
                            if w:
                                dve.wait_ge(v_tap, 3 * i + (3 * it0 + w + 1))
                            for f in range(4):
                                c = lambda m: taps[:, m, i, f:f + 1]
                                if w == 0:
                                    last = dve.tensor_scalar(ybuf[:, f, :], gbuf[:, f, 0:T], c(0), c(3), ALU.mult, ALU.add)
                                else:
                                    last = dve.scalar_tensor_tensor(ybuf[:, f, :], gbuf[:, f, w:w + T], c(w),
                                                                    ybuf[:, f, :], ALU.mult, ALU.add)
                            last.then_inc(v_tap, 1)
                        if j == 13:
                            dve.wait_ge(a_silu, i + (it0 + 1))
                            tt(ybuf[:, :, :], ybuf[:, :, :], rms4, ALU.mult).then_inc(v_yr, 1)
                        if j == 15:
                            dve.wait_ge(a_u, i + (it0 + 1))
                            tt(hf[:, :, :], hf[:, :, :], ps[:, 4:8, T:2 * T], ALU.add).then_inc(v_up, 1)
                            dve.wait_ge(v_up, i + (it0 + 2))
                            dve.wait_ge(v_yr, i + (it0 + 1))
                            tt(hf[:, :, :], hf[:, :, :], ybuf[:, :, :], ALU.mult).then_inc(v_gu, 1)
                            dve.wait_ge(a_gh, i + (it0 + 1))
                            tt(gs[:, i, :, 1, :], hf[:, :, :], gs[:, i, :, 0, :].bitcast(F32), ALU.subtract).then_inc(v_glo, 1)

                up_group(0)
                with dve.Fori(1, UP_GROUPS) as i:
                    up_group(i)
                base += 16 * UP_GROUPS
                xb = X_DOWN1 if layer else X_DOWN0
                x1 = 8 + 12 * layer
                if layer == 0:
                    dve.wait_ge(p_ss, 2)
                    dve.memset(ssacc[:, :, :], 0.0).then_inc(v_set, 1)
                    dve.wait_ge(v_set, 5)
                    with dve.Fori(0, 2) as i:
                        for j in range(2 * DOWN_UNITS):
                            conv_lo_loop(base + RAW, 2 * DOWN_UNITS, i, j)
                            if j % DOWN_UNITS == DOWN_UNITS - 1:
                                g = j // DOWN_UNITS
                                dve.wait_ge(unit_done, 2 * DOWN_UNITS * i + (base + j + 1))
                                xs = xT[:, :, :].rearrange("p (i g k) t -> p i g k t", i=2, g=2)[:, i, g, :, :]
                                residual(None, 2 * i + (x1 + g + 1), xs, 4 * g, 4)
                                for h in range(2):
                                    n = xb + 2 * g + h
                                    dve.wait_ge(a_sqx, 4 * i + (n + 1))
                                    dve.wait_ge(v_ss, 4 * i + n)
                                    tt(ssacc[:, :, :], ssacc[:, :, :], sqt[:, n % 2, :, :], ALU.add).then_inc(v_ss, 1)
                                for q in range(4):
                                    dve.wait_ge(a_hh, 8 * i + (2 * KT + 4 * g + q + 1))
                                    x_tile, gain, h_tile = down_tile(i, g, q)
                                    prep_lo(2, None, x_tile, gain, h_tile)
                else:
                    for u in range(base, U_END):
                        if u + RAW < U_END:
                            conv_lo(u + RAW)
                        j = u - base
                        if j % DOWN_UNITS == DOWN_UNITS - 1:
                            g = j // DOWN_UNITS
                            dve.wait_ge(unit_done, u + 1)
                            residual(None, x1 + g + 1, xT[:, 4 * g:4 * g + 4, :], 4 * (g % 2), 4)

            for free in (v_gate, v_up, v_tap, v_glo):
                dve.sem_inc(free, 1)
            dve.memset(eps[:, :], EPS).then_inc(v_set, 1)
            dve.memset(gbuf[:, :, 0:2], 0.0).then_inc(v_set, 1)
            dve.memset(ones_t[:, :], 1.0).then_inc(v_set, 1)
            dve.memset(fb[96:128, :], 0.0).then_inc(v_set, 1)
            dve.wait_ge(v_set, 4)

            def tables():
                dve.wait_ge(p_tab, 1)
                dve.tensor_copy(gains[:, :, :], ps[:, 7, 0:4 * KT].rearrange("p (n k) -> p n k", k=KT)).then_inc(v_tab, 1)
                dve.tensor_copy(conv[:, :, :, :], ps[:, 6, 0:8 * FT].rearrange("p (l w f) -> p l w f", l=LAYERS, w=4)).then_inc(v_tab, 1)

            for n in range(8):
                dve.wait_ge(p_x, n + 1)
                dve.tensor_copy(xT[:, 2 * n:2 * n + 2, :],
                                ps[:, n % 6, :].rearrange("p (k t) -> p k t", k=2)).then_inc(v_x, 1)
                if 3 <= n <= 5:
                    add_square(X_LOAD + n - 3)
                if n == 5:
                    tables()
                    conv_lo(0)
                if n == 7:
                    for pair in range(8):
                        prep(0, pair)
                        if pair == 3:
                            conv_lo(1)
            for u in range(2, RAW):
                conv_lo(u)
            for n in range(3, 8):
                add_square(X_LOAD + n)
            for s in fox_plan() + out_plan(U_FOX_OUT):
                step(s)
            ffn(0)
            dve.wait_ge(unit_done, U_SWA)
            dve.memset(pr[:, :, 1, 0:CHUNK], 0.0).then_inc(v_set, 1)
            for s in swa_plan() + out_plan(U_SWA_OUT):
                step(s)
            ffn(1)
            for n in range(0, 8, 2):
                dve.wait_ge(p_out, n + 1)
                dve.tensor_copy(xin[:, 0, 256 * n:256 * n + 512], ps[:, n, :]).then_inc(v_out, 1)

        @block.tensor
        def _(pe):
            def mm_w(slot, kj, f, width, moving, bank, first, last):
                c = (kj * width + f) * P
                hi = lambda: pe.matmul(ps[:, bank, :], whi[slot][:, c:c + P], moving.rearrange("p h t -> p (h t)"),
                                       start=first, stop=last)
                lo = lambda: pe.matmul(ps[:, bank, 0:T], wlo[slot][:, c:c + P], moving[:, 0, :], start=False, stop=False)
                if last:
                    lo()
                    return hi()
                hi()
                return lo()

            def unit(s):
                _, u, kind, g, j = s
                pe.wait_ge(lo_ready, u + 1)
                slot, b = u % RAW, proj_banks(u)
                if j == 0:
                    free_bank(s)
                if kind == "f":
                    for kj in range(8):
                        k = 8 * j + kj
                        pe.wait_ge(v_hl, k + 1)
                        last = mm_w(slot, kj, 0, 1, hs[:, k, :, :], b, k == 0, k == KT - 1)
                elif kind == "v":
                    for kj in range(4):
                        k = 4 * j + kj
                        w0 = kj * 256
                        for t in range(TT):
                            tok = slice(t * P, (t + 1) * P)
                            o = ps[:, b, t * 256:(t + 1) * 256]
                            pe.matmul(o, hs[:, k, 1, tok], whi[slot][:, w0:w0 + 256],
                                      start=k == 0 and t == 0, stop=False)
                            pe.matmul(o, hs[:, k, 0, tok], wlo[slot][:, w0:w0 + 256], start=False, stop=False)
                            last = pe.matmul(o, hs[:, k, 0, tok], whi[slot][:, w0:w0 + 256], start=False,
                                             stop=k == KT - 1 and t == TT - 1)
                else:
                    for kj in range(4):
                        k = 4 * j + kj
                        if kind == "o" and g <= 1:
                            pe.wait_ge(v_ol, (0 if u < U_FFN[0] else FOX_H) + k + 1)
                        if kind != "o" and u >= U_SWA:
                            pe.wait_ge(v_hl, 2 * KT + k + 1)
                        for f in range(2):
                            src = oT if kind == "o" else hs
                            last = mm_w(slot, kj, f, 2, src[:, k, :, :], b + f, k == 0, k == KT - 1)
                last.then_inc(unit_done, 1)

            def free_bank(s):
                _, u, kind, g, j = s
                if kind == "f":
                    pe.wait_ge(v_tab, 2)
                elif kind in "qkv" and u < U_FOX_OUT:
                    n = (u - U_FOX) // 4
                    if n < 2:
                        pe.wait_ge(v_x, 8)
                    else:
                        m = n - 2
                        if m % 3 == 2:
                            pe.wait_ge(a_v, m // 3 + 1)
                        else:
                            pe.wait_ge(v_q1, 2 * (m // 3) + m % 3 + 1)
                elif kind in "qkv":
                    if u < U_SWA + 4:
                        pe.wait_ge(v_x, X_DOWN0 + 6)
                    elif kind == "v":
                        pe.wait_ge(v_x, X_DOWN0 + 8)
                    else:
                        pe.wait_ge(v_q1, FOX_N + (1, 1, 2)[g] if g < 3 else FOX_N + 1 + g)
                else:
                    fox = u < U_FFN[0]
                    xb = X_OUT0 if fox else X_OUT1
                    if g == 0:
                        pe.wait_ge(v_qs, FOX_N if fox else FOX_N + 1 + SWA_GROUPS)
                    elif g == 1:
                        pe.wait_ge(a_v, FOX_PAIRS)
                        if not fox:
                            pe.wait_ge(v_ol, 2 * FOX_H)
                        pe.wait_ge(v_qs, FOX_N if fox else FOX_N + 1 + SWA_GROUPS)
                    else:
                        pe.wait_ge(v_x, xb + g - 1)

            bank7 = [(v_tab, 2)]

            def take_bank7(by):
                pe.wait_ge(*bank7[0])
                bank7[0] = by

            def step(s):
                kind, n = s[0], s[1]
                if kind == "unit":
                    unit(s)
                elif kind == "stats":
                    mean_square(n)
                elif kind == "rcol":
                    pe.wait_ge(a_r, n + 1)
                    for t in range(TT):
                        last = pe.matmul(ps[:, stats_bank(n), T + t:T + t + 1], rbc[:, t * P:(t + 1) * P], ident[:, 0:1],
                                         start=True, stop=True)
                    last.then_inc(p_rc, 1)
                elif kind == "ssq":
                    pe.wait_ge(a_sq, n + 1)
                    take_bank7((a_ln, n + 1))
                    pe.wait_ge(f_land if n < FOX_N else s_land, (6 if n < FOX_N else 11) * 16)
                    pe.matmul(ps[:, 7, :], mean_h[:, :], sq[:, :, :].rearrange("p f t -> p (f t)"),
                              start=True, stop=True).then_inc(p_ssq, 1)
                elif kind == "rot":
                    pe.wait_ge(v_qn, n + 1)
                    take_bank7((v_rope, n - FOX_N + 1))
                    pe.matmul(ps[:, 7, :], swap[:, :], tq[:, :, :].rearrange("p f t -> p (f t)"),
                              start=True, stop=True).then_inc(p_rot, 1)
                elif kind == "S":
                    scores(n)
                elif kind == "PT":
                    pe.wait_ge(a_ex, n + 1)
                    if n > 0:
                        pe.wait_ge(a_pt, n)
                    for a in range(3):
                        last = pe.transpose(ps[:, 6, a * P:(a + 1) * P], pr[:, n % 4, a, :], ident[:, :])
                    last.then_inc(p_pt, 1)
                elif kind == "PV":
                    fox = n < FOX_H
                    pe.wait_ge(a_pt, n + 1)
                    pe.wait_ge(a_v, n // 2 + 1 if fox else FOX_PAIRS + 1)
                    dh = FOX_D if fox else SWA_D
                    c = FOX_D * (n % 2) if fox else SWA_D * ((n - FOX_H) // 8)
                    v = (n // 2) % 2 if fox else FOX_PAIRS % 2
                    o = lambda t: ps[:, head_bank(n), t * dh:(t + 1) * dh]
                    pe.matmul(o(0), pT[:, n % 4, 0, :], vt[:, v, 0, c:c + dh], start=True, stop=True)
                    pe.matmul(o(1), pT[:, n % 4, 1, :], vt[:, v, 0, c:c + dh], start=True, stop=False)
                    pe.matmul(o(1), pT[:, n % 4, 2, :], vt[:, v, 1, c:c + dh], start=False, stop=True).then_inc(p_pv, 1)
                elif kind == "OT":
                    pe.wait_ge(v_on, n + 1)
                    if n >= FOX_H:
                        take_bank7((v_ol, out_tile(n)[0] + 1))
                    for t in range(TT):
                        last = pe.transpose(ps[:, out_bank(n), T + t * P:T + (t + 1) * P], on[:, on_slot(n), t, :], ident[:, :])
                    last.then_inc(p_ot, 1)

            def scores(n):
                b = head_bank(n)
                if n < FOX_H:
                    pair = n // 2
                    pe.wait_ge(v_qn, 2 * pair + 2)
                    pe.wait_ge(v_c, 1)
                    pe.wait_ge(a_cst, 1)
                    if n >= 2:
                        pe.wait_ge(v_ol, n - 1)
                    q, k = qn[:, pair % 2, n % 2, :], kn[:, pair % 2, n % 2, :]
                    for t in range(TT):
                        keys = (t + 1) * P
                        o = ps[:, b, P * t:P * t + keys]
                        pe.matmul(o, q[:, t * P:(t + 1) * P], k[:, 0:keys], start=True, stop=False)
                        sel = ident[96:128, 112 + n:113 + n].to_broadcast([32, P])
                        pe.matmul(o, sel, nc_k[96:128, 0:keys], start=False, stop=False)
                        last = pe.matmul(ps[:, b, P * t + keys - P:P * t + keys], ident_r[:, :], mask_r[:, 0:P],
                                         start=False, stop=True)
                else:
                    h = n - FOX_H
                    m = h // 4 + 1
                    pe.wait_ge(v_qr, m + 1)
                    pe.wait_ge(a_kd, 1)
                    pe.wait_ge(a_cst, 2)
                    if h >= 4:
                        pe.wait_ge(v_on, n - 3)
                    else:
                        pe.wait_ge(v_ol, FOX_H)
                        pe.wait_ge(a_v, FOX_PAIRS + 1)
                        pe.wait_ge(v_q1, FOX_N + 3)
                    half = slice(SWA_D * (h % 2), SWA_D * (h % 2) + SWA_D)
                    q, k = qn[half, m % 2, h % 4 // 2, :], kdup[half, h // 8, :]
                    for t, (o0, k0, keys) in enumerate(((0, 0, P), (P, CHUNK, P + CHUNK))):
                        o = ps[:, b, o0:o0 + keys]
                        pe.matmul(o, q[:, t * P:(t + 1) * P], k[:, k0:k0 + keys], start=True, stop=False)
                        last = pe.matmul(o, ident_r[:, :], mask_r[:, o0:o0 + keys], start=False, stop=True)
                last.then_inc(p_s, 1)

            def mean_square(n):
                b = stats_bank(n)
                pe.wait_ge(v_ss, 8 * (n + 1))
                pe.wait_ge(f_land, 6 * 16)
                pe.matmul(ps[:, b, 0:T], mean_d[:, :], ssacc[:, 0, :], start=True, stop=False)
                pe.matmul(ps[:, b, 0:T], mean_d[:, :], ssacc[:, 1, :], start=False, stop=True).then_inc(p_ss, 1)

            def ffn(layer):
                base, it0, n0 = U_FFN[layer], UP_GROUPS * layer, KT * (2 * layer + 1)
                pe.wait_ge(v_x, (X_OUT1 if layer else X_OUT0) + 7)

                def up_group(i, first):
                    for j in range(16):
                        b = 4 * (j // 8)
                        if j == 0:
                            pe.wait_ge(v_gate, i + (it0 + 1))
                        if j == 8:
                            pe.wait_ge(v_up, i + (it0 + 1))
                        if first and j == 4:
                            mean_square(2 * layer + 1)
                        if first and j == 8:
                            pe.wait_ge(a_rln, 2 * layer + 2)
                        pe.wait_ge(lo_ready, 16 * i + (base + j + 1))
                        slot = (base + j) % RAW
                        order = [(kj, f) for kj in range(2) for f in range(4)]
                        if first and j == 0:
                            order = [(kj, f) for h in range(2) for kj in range(2) for f in (2 * h, 2 * h + 1)]
                        for kj, f in order:
                            k = 2 * (j % 8) + kj
                            if j < 8:
                                pe.wait_ge(v_hl, n0 + k + 1)
                            if first and j == 0 and kj == 0 and f == 2:
                                pe.wait_ge(v_x, (X_OUT1 if layer else X_OUT0) + 8)
                            last = mm_w(slot, kj, f, 4, hs[:, k, :, :], b + f, k == 0, k == KT - 1)
                        last.then_inc(unit_done, 1)

                up_group(0, True)
                with pe.Fori(1, UP_GROUPS) as i:
                    up_group(i, False)
                base += 16 * UP_GROUPS
                xb = X_DOWN1 if layer else X_DOWN0
                pe.wait_ge(v_gate, it0 + UP_GROUPS + 1)
                with pe.Fori(0, 2) as i:
                    for j in range(2 * DOWN_UNITS):
                        g = j // DOWN_UNITS
                        if j % DOWN_UNITS == 0:
                            if g == 1:
                                pe.wait_ge(v_up, it0 + UP_GROUPS + 1)
                            pe.wait_ge(v_x, 4 * i + (xb + 2 * g - 2))
                        pe.wait_ge(lo_ready, 2 * DOWN_UNITS * i + (base + j + 1))
                        slot = (base + j) % RAW
                        for kj in range(2):
                            k = 2 * (j % DOWN_UNITS) + kj
                            if g == 0:
                                pe.wait_ge(v_glo, it0 + k // 4 + 2)
                            for f in range(4):
                                last = mm_w(slot, kj, f, 4, gs[:, k // 4, k % 4, :, :], 4 * g + f, k == 0, k == FT - 1)
                        last.then_inc(unit_done, 1)

            pe.wait_ge(i_land, 16)
            for n in range(8):
                if n % 2 == 0:
                    pe.wait_ge(x_land[n // 2], TT * 16)
                if n == 5:
                    pe.wait_ge(c_land, 6 * 16)
                    for m in range(2 * LAYERS):
                        pe.transpose(ps[:, 7, m * KT:(m + 1) * KT], grow[:, m, :], ident[0:KT, 0:KT])
                    for m in range(4 * LAYERS):
                        last = pe.transpose(ps[:, 6, m * FT:(m + 1) * FT], small[:, m, :], ident[0:FT, 0:FT])
                    last.then_inc(p_tab, 1)
                if n >= 6:
                    pe.wait_ge(v_x, n - 5)
                for k in range(2):
                    for t in range(TT):
                        f = 2 * n + k
                        last = pe.transpose(ps[:, n % 6, k * T + t * P:k * T + (t + 1) * P], xin[:, t, f * P:(f + 1) * P], ident[:, :])
                last.then_inc(p_x, 1)
            for s in fox_plan():
                step(s)
            for s in out_plan(U_FOX_OUT):
                step(s)
            ffn(0)
            for s in swa_plan() + out_plan(U_SWA_OUT):
                step(s)
            ffn(1)
            for n in range(8):
                q, t = n // 2, n % 2
                pe.wait_ge(v_x, X_DOWN1 + (6 if n < 4 else 8))
                for k in range(4):
                    last = pe.transpose(ps[:, n, k * P:(k + 1) * P], xT[:, 4 * q + k, t * P:(t + 1) * P], ident[:, :])
                last.then_inc(p_out, 1)


_INS = ["x", "attn_norm", "ffn_norm", "fox_w_in", "fox_f_bias", "fox_q_norm", "fox_k_norm", "fox_w_out",
        "swa_w_in", "swa_q_norm", "swa_k_norm", "swa_sinks", "swa_w_out", "ffn_w_up", "ffn_conv_w",
        "ffn_conv_b", "ffn_w_down"]


def kernel(**inputs):
    import concourse.bacc as bacc
    from concourse.bass_utils import run_bass_kernel_spmd

    nc = bacc.Bacc("TRN2", target_bir_lowering=False, num_devices=1)
    arrays, args = {}, []
    for name in _INS:
        a = np.ascontiguousarray(inputs[name])
        arrays[f"in_{name}"] = a
        args.append(nc.dram_tensor(f"in_{name}", a.shape, mybir.dt.from_np(a.dtype), kind="ExternalInput").ap())
    args.append(nc.dram_tensor("out_x", (1, T, D), F32, kind="ExternalOutput").ap())
    trunk(nc, *args)
    r = run_bass_kernel_spmd(nc, [arrays], core_ids=[0])
    return r.results[0]["out_x"]
```
